# Optimizing a Trainium2 kernel written in Bass

```python
import jax, jax.numpy as jnp
from jax import lax
import numpy as np
import math

D_MODEL = 1024
BATCH = 1
SEQ = 512
DEPTH = 2

N_HEADS = 16
HEAD_DIM = D_MODEL // N_HEADS
D_FF = -(-8 * D_MODEL // (3 * 256)) * 256
N_A_LAYERS = DEPTH // 2
N_B_LAYERS = DEPTH - N_A_LAYERS
BLOCK = 128
ROPE_THETA = 10000.0
NORM_EPS = 1e-6
DILATED_BRANCHES = ((128, 1), (512, 4), (2048, 16))


def _rmsnorm(h, g):
    hf = h.astype(jnp.float32)
    y = hf * lax.rsqrt(jnp.mean(hf * hf, axis=-1, keepdims=True) + NORM_EPS)
    return (y * g.astype(jnp.float32)).astype(h.dtype)

def _rope(a):
    s, d = a.shape[1], a.shape[3]
    inv_freq = ROPE_THETA ** (-jnp.arange(0, d, 2, dtype=jnp.float32) / d)
    ang = jnp.arange(s, dtype=jnp.float32)[:, None] * inv_freq[None, :]
    cos = jnp.cos(ang)[:, None, :]
    sin = jnp.sin(ang)[:, None, :]
    af = a.astype(jnp.float32)
    a1, a2 = af[..., : d // 2], af[..., d // 2:]
    return jnp.concatenate([a1 * cos - a2 * sin, a2 * cos + a1 * sin], axis=-1).astype(a.dtype)

def _swiglu(h, w_gate, w_up, w_down):
    return (jax.nn.silu(h @ w_gate) * (h @ w_up)) @ w_down

def _stick_breaking(q, k, v):
    b, s, h, d = q.shape
    nq = s // BLOCK
    scale = d ** -0.5
    kh = k.transpose(0, 2, 1, 3)
    vh = v.transpose(0, 2, 1, 3)
    qblk = q.reshape(b, nq, BLOCK, h, d).transpose(1, 0, 3, 2, 4)
    key_pos = jnp.arange(s)

    def one_block(args):
        qb, bi = args
        qpos = bi * BLOCK + jnp.arange(BLOCK)
        strict = key_pos[None, :] < qpos[:, None]
        z = jnp.einsum('bhqd,bhkd->bhqk', qb, kh).astype(jnp.float32) * scale
        log_stay = jnp.where(strict, jax.nn.log_sigmoid(-z), 0.0)
        log_after = lax.cumsum(log_stay, axis=3, reverse=True) - log_stay
        w = jnp.where(strict, jnp.exp(jax.nn.log_sigmoid(z) + log_after), 0.0)
        return jnp.einsum('bhqk,bhkd->bhqd', w, vh.astype(jnp.float32)).astype(q.dtype)

    out = lax.map(one_block, (qblk, jnp.arange(nq)))
    return out.transpose(1, 0, 3, 2, 4).reshape(b, s, h, d)

def _to_blocks(a, r):
    b, s, h, d = a.shape
    n = s // r
    nb = -(-n // BLOCK)
    a = a.reshape(b, n, r, h, d).transpose(0, 2, 3, 1, 4)
    a = jnp.pad(a, ((0, 0), (0, 0), (0, 0), (0, nb * BLOCK - n), (0, 0)))
    return a.reshape(b, r, h, nb, BLOCK, d)

def _from_blocks(a, s):
    b, r, h, nb, blk, e = a.shape
    n = s // r
    a = a.reshape(b, r, h, nb * blk, e)[:, :, :, :n]
    return a.transpose(0, 3, 1, 2, 4).reshape(b, s, h, e)

def _dilated_branch(qb, kb, vb, steps):
    nb = qb.shape[3]
    scale = qb.shape[-1] ** -0.5
    k_prev = jnp.concatenate([jnp.zeros_like(kb[:, :, :, :1]), kb[:, :, :, :-1]], axis=3)
    v_prev = jnp.concatenate([jnp.zeros_like(vb[:, :, :, :1]), vb[:, :, :, :-1]], axis=3)
    k_band = jnp.concatenate([k_prev, kb], axis=4)
    v_band = jnp.concatenate([v_prev, vb], axis=4)
    z = jnp.einsum('brhnqd,brhnkd->brhnqk', qb, k_band).astype(jnp.float32) * scale
    qi = jnp.arange(BLOCK)[:, None]
    kj = jnp.arange(2 * BLOCK)[None, :]
    dist = BLOCK + qi - kj
    key_idx = (jnp.arange(nb)[:, None, None] - 1) * BLOCK + kj[None]
    valid = (dist >= 0)[None] & (dist <= steps)[None] & (key_idx >= 0)
    z = jnp.where(valid, z, -jnp.inf)
    m = jnp.max(z, axis=-1, keepdims=True)
    p = jnp.exp(z - m)
    den = jnp.sum(p, axis=-1, keepdims=True)
    o = jnp.einsum('brhnqk,brhnkd->brhnqd', p, v_band.astype(jnp.float32)) / den
    lse = m + jnp.log(den)
    return o, lse

def _dilated_attention(q, kv_blocks):
    s = q.shape[1]
    outs, lses = [], []
    for (window, r), (kb, vb) in zip(DILATED_BRANCHES, kv_blocks):
        o, lse = _dilated_branch(_to_blocks(q, r), kb, vb, window // r)
        outs.append(_from_blocks(o, s))
        lses.append(_from_blocks(lse, s))
    wts = jax.nn.softmax(jnp.stack(lses, axis=0), axis=0)
    return jnp.sum(wts * jnp.stack(outs, axis=0), axis=0).astype(q.dtype)

def first_inputs(seed: int = 0) -> dict:
    key = jax.random.key(seed)
    ks = jax.random.split(key, 14)
    d, f = D_MODEL, D_FF
    nrm = lambda k, shape, fan: jax.random.normal(k, shape, jnp.float32) * fan ** -0.5
    gain = lambda k, shape: 1.0 + 0.02 * jax.random.normal(k, shape, jnp.float32)
    return {
        "x": jax.random.normal(ks[0], (BATCH, SEQ, d), jnp.float32),
        "norm_mix": gain(ks[1], (DEPTH, d)),
        "w_qkv_a": nrm(ks[2], (N_A_LAYERS, d, 3 * d), d),
        "w_o_a": nrm(ks[3], (N_A_LAYERS, d, d), d),
        "norm_kv": gain(ks[4], (d,)),
        "w_kv": nrm(ks[5], (d, 2 * d), d),
        "w_q_b": nrm(ks[6], (N_B_LAYERS, d, d), d),
        "w_o_b": nrm(ks[7], (N_B_LAYERS, d, d), d),
        "norm_ffn": gain(ks[8], (DEPTH, d)),
        "w_gate": nrm(ks[9], (DEPTH, d, f), d),
        "w_up": nrm(ks[10], (DEPTH, d, f), d),
        "w_down": nrm(ks[11], (DEPTH, f, d), f),
        "norm_final": gain(ks[12], (d,)),
    }

def first_block(x, norm_mix, w_qkv_a, w_o_a, norm_kv, w_kv, w_q_b, w_o_b,
              norm_ffn, w_gate, w_up, w_down, norm_final):
    b, s, d = x.shape
    h = x
    kv_blocks = None
    for layer in range(DEPTH):
        hn = _rmsnorm(h, norm_mix[layer])
        if layer < N_A_LAYERS:
            q, k, v = jnp.split(hn @ w_qkv_a[layer], 3, axis=-1)
            q = q.reshape(b, s, N_HEADS, HEAD_DIM)
            k = k.reshape(b, s, N_HEADS, HEAD_DIM)
            v = v.reshape(b, s, N_HEADS, HEAD_DIM)
            o = _stick_breaking(q, k, v).reshape(b, s, d)
            h = h + o @ w_o_a[layer]
        else:
            j = layer - N_A_LAYERS
            if layer == N_A_LAYERS:
                kv = _rmsnorm(h, norm_kv) @ w_kv
                ks_, vs_ = jnp.split(kv, 2, axis=-1)
                ks_ = _rope(ks_.reshape(b, s, N_HEADS, HEAD_DIM))
                vs_ = vs_.reshape(b, s, N_HEADS, HEAD_DIM)
                kv_blocks = tuple((_to_blocks(ks_, r), _to_blocks(vs_, r))
                                  for (_, r) in DILATED_BRANCHES)
            q = _rope((hn @ w_q_b[j]).reshape(b, s, N_HEADS, HEAD_DIM))
            o = _dilated_attention(q, kv_blocks).reshape(b, s, d)
            h = h + o @ w_o_b[j]
        h = h + _swiglu(_rmsnorm(h, norm_ffn[layer]), w_gate[layer], w_up[layer], w_down[layer])
    return _rmsnorm(h, norm_final)


N_A_LAYERS_2 = DEPTH // 2
N_B_LAYERS_2 = DEPTH - N_A_LAYERS_2
HG_HEADS = 8
HG_DIM = D_MODEL // HG_HEADS
HG_CHUNK = 32
SW_Q_HEADS = 16
SW_KV_HEADS = 4
SW_HEAD_DIM = D_MODEL // SW_Q_HEADS
SW_GROUP = SW_Q_HEADS // SW_KV_HEADS
SW_WINDOW = 128
REL_BUCKETS = 32
REL_MAX_DIST = 128
FFN_DIM = 2816
CONV_WIDTH = 3
ALPHA = (2.0 * DEPTH) ** 0.25
BETA = (8.0 * DEPTH) ** -0.25
LN_EPS = 1e-5
RMS_EPS = 1e-6


def layer_norm(x, g, b):
    xf = x.astype(jnp.float32)
    mu = xf.mean(-1, keepdims=True)
    var = jnp.square(xf - mu).mean(-1, keepdims=True)
    y = (xf - mu) * lax.rsqrt(var + LN_EPS) * g.astype(jnp.float32) + b.astype(jnp.float32)
    return y.astype(x.dtype)

def hgrn2_chunkwise(q, k, v, log_f):
    B, S, H, Dk = q.shape
    Dv = v.shape[-1]
    n = S // HG_CHUNK

    def chunks(a):
        return a.reshape(B, n, HG_CHUNK, H, a.shape[-1]).transpose(1, 0, 3, 2, 4)

    qc, kc, vc = chunks(q), chunks(k), chunks(v)
    bc = jnp.cumsum(chunks(log_f), axis=3)
    causal = jnp.tril(jnp.ones((HG_CHUNK, HG_CHUNK), dtype=bool))[:, :, None]

    def step(state, inp):
        q_, k_, v_, b_ = inp
        o_inter = jnp.einsum('bhtk,bhkv->bhtv', q_ * jnp.exp(b_), state)
        diff = b_[:, :, :, None, :] - b_[:, :, None, :, :]
        decay = jnp.where(causal, jnp.exp(jnp.minimum(diff, 0.0)), 0.0)
        scores = jnp.einsum('bhtsk,bhsk->bhts', q_[:, :, :, None, :] * decay, k_)
        o = o_inter + jnp.einsum('bhts,bhsv->bhtv', scores, v_)
        b_last = b_[:, :, -1, :]
        k_dec = k_ * jnp.exp(b_last[:, :, None, :] - b_)
        state = jnp.exp(b_last)[..., None] * state + jnp.einsum('bhsk,bhsv->bhkv', k_dec, v_)
        return state, o

    state0 = jnp.zeros((B, H, Dk, Dv), jnp.float32)
    _, o = lax.scan(step, state0, (qc, kc, vc, bc))
    return o.transpose(1, 0, 3, 2, 4).reshape(B, S, H, Dv)

def hgrn2_mixer(h, w_in, lower_bound, g_norm_w, w_out):
    B, S, D = h.shape
    q, f, i, g = jnp.split(h @ w_in, 4, axis=-1)

    def heads(a):
        return a.reshape(B, S, HG_HEADS, HG_DIM).astype(jnp.float32)

    lb = lower_bound.astype(jnp.float32).reshape(HG_HEADS, HG_DIM)
    fg = lb + (1.0 - lb) * jax.nn.sigmoid(heads(f))
    o = hgrn2_chunkwise(jax.nn.silu(heads(q)), 1.0 - fg, heads(i), jnp.log(fg))
    o = o * lax.rsqrt(jnp.mean(jnp.square(o), -1, keepdims=True) + RMS_EPS)
    o = o * g_norm_w.astype(jnp.float32) * jax.nn.silu(heads(g))
    return o.reshape(B, S, D).astype(h.dtype) @ w_out

def t5_causal_bucket(dist):
    exact = REL_BUCKETS // 2
    d = jnp.maximum(dist, 1).astype(jnp.float32)
    log_b = exact + (jnp.log(d / exact) / math.log(REL_MAX_DIST / exact)
                     * (REL_BUCKETS - exact)).astype(jnp.int32)
    return jnp.where(dist < exact, dist, jnp.minimum(log_b, REL_BUCKETS - 1))

def banded_bias_and_mask(rel_table, n_blocks):
    t = jnp.arange(SW_WINDOW)[:, None] + SW_WINDOW
    s = jnp.arange(2 * SW_WINDOW)[None, :]
    dist = t - s
    bias = rel_table[t5_causal_bucket(jnp.maximum(dist, 0))].transpose(2, 0, 1)
    band = (dist >= 0) & (dist < SW_WINDOW)
    has_prev = (jnp.arange(n_blocks) > 0)[:, None, None]
    mask = band[None] & (has_prev | (s >= SW_WINDOW)[None])
    return bias, mask

def swa_sink_mixer(h, k, v, w_q, sinks, bias, mask, w_out):
    B, S, D = h.shape
    nb = S // SW_WINDOW
    q = (h @ w_q).reshape(B, nb, SW_WINDOW, SW_KV_HEADS, SW_GROUP, SW_HEAD_DIM)

    def with_prev(a):
        ab = a.reshape(B, nb, SW_WINDOW, SW_KV_HEADS, SW_HEAD_DIM)
        prev = jnp.pad(ab, ((0, 0), (1, 0), (0, 0), (0, 0), (0, 0)))[:, :-1]
        return jnp.concatenate([prev, ab], axis=2)

    kk, vv = with_prev(k), with_prev(v)
    scale = SW_HEAD_DIM ** -0.5
    logits = jnp.einsum('bntgrd,bnsgd->bngrts', q, kk).astype(jnp.float32) * scale
    logits = logits + bias.astype(jnp.float32).reshape(SW_KV_HEADS, SW_GROUP, SW_WINDOW, 2 * SW_WINDOW)
    logits = jnp.where(mask[None, :, None, None], logits, -jnp.inf)
    sink = sinks.astype(jnp.float32).reshape(1, 1, SW_KV_HEADS, SW_GROUP, 1)
    m = jnp.maximum(logits.max(-1), sink)
    p = jnp.exp(logits - m[..., None])
    denom = p.sum(-1) + jnp.exp(sink - m)
    o = jnp.einsum('bngrts,bnsgd->bntgrd', p, vv.astype(jnp.float32))
    o = o / jnp.moveaxis(denom, -1, 2)[..., None]
    return o.reshape(B, S, D).astype(h.dtype) @ w_out

def conv_ffn(h, w_in, conv_w, conv_b, w_out):
    u = h @ w_in
    C = u.shape[-1]
    u = lax.conv_general_dilated(u, conv_w[:, None, :], window_strides=(1,),
                                 padding=[(CONV_WIDTH - 1, 0)],
                                 dimension_numbers=('NWC', 'WIO', 'NWC'),
                                 feature_group_count=C) + conv_b
    a, b = jnp.split(u, 2, axis=-1)
    return (jax.nn.silu(a) * b) @ w_out

def second_inputs(seed: int = 0) -> dict:
    key = jax.random.key(seed)
    ks = jax.random.split(key, 24)
    D, F = D_MODEL, FFN_DIM
    kv_dim = SW_KV_HEADS * SW_HEAD_DIM
    nrm = jax.random.normal

    x = nrm(ks[0], (BATCH, SEQ, D), jnp.float32)

    hgrn_w_in = nrm(ks[1], (N_A_LAYERS_2, D, 4 * D), jnp.float32) * D ** -0.5
    hgrn_w_in = hgrn_w_in.at[..., 2 * D:3 * D].multiply(BETA)
    hgrn_lb_logits = nrm(ks[2], (N_A_LAYERS_2 + 1, D), jnp.float32) * 0.5
    hgrn_gnorm_w = 1.0 + 0.02 * nrm(ks[3], (N_A_LAYERS_2, HG_DIM), jnp.float32)
    hgrn_w_out = nrm(ks[4], (N_A_LAYERS_2, D, D), jnp.float32) * D ** -0.5 * BETA

    swa_w_q = nrm(ks[5], (N_B_LAYERS_2, D, D), jnp.float32) * D ** -0.5
    swa_sinks = nrm(ks[6], (N_B_LAYERS_2, SW_Q_HEADS), jnp.float32) * 0.5
    swa_w_out = nrm(ks[7], (N_B_LAYERS_2, D, D), jnp.float32) * D ** -0.5 * BETA
    shared_w_kv = nrm(ks[8], (D, 2 * kv_dim), jnp.float32) * D ** -0.5
    shared_w_kv = shared_w_kv.at[:, kv_dim:].multiply(BETA)
    rel_bias = nrm(ks[9], (REL_BUCKETS, SW_Q_HEADS), jnp.float32) * 0.5

    ffn_w_in = nrm(ks[10], (DEPTH, D, 2 * F), jnp.float32) * D ** -0.5 * BETA
    ffn_conv_w = nrm(ks[11], (DEPTH, CONV_WIDTH, 2 * F), jnp.float32) * CONV_WIDTH ** -0.5
    ffn_conv_b = nrm(ks[12], (DEPTH, 2 * F), jnp.float32) * 0.02
    ffn_w_out = nrm(ks[13], (DEPTH, F, D), jnp.float32) * F ** -0.5 * BETA

    ln_mix_g = 1.0 + 0.02 * nrm(ks[14], (DEPTH, D), jnp.float32)
    ln_mix_b = 0.02 * nrm(ks[15], (DEPTH, D), jnp.float32)
    ln_ffn_g = 1.0 + 0.02 * nrm(ks[16], (DEPTH, D), jnp.float32)
    ln_ffn_b = 0.02 * nrm(ks[17], (DEPTH, D), jnp.float32)

    return {"x": x, "hgrn_w_in": hgrn_w_in, "hgrn_lb_logits": hgrn_lb_logits,
            "hgrn_gnorm_w": hgrn_gnorm_w, "hgrn_w_out": hgrn_w_out,
            "swa_w_q": swa_w_q, "swa_sinks": swa_sinks, "swa_w_out": swa_w_out,
            "shared_w_kv": shared_w_kv, "rel_bias": rel_bias,
            "ffn_w_in": ffn_w_in, "ffn_conv_w": ffn_conv_w, "ffn_conv_b": ffn_conv_b,
            "ffn_w_out": ffn_w_out, "ln_mix_g": ln_mix_g, "ln_mix_b": ln_mix_b,
            "ln_ffn_g": ln_ffn_g, "ln_ffn_b": ln_ffn_b}

def second_block(x, hgrn_w_in, hgrn_lb_logits, hgrn_gnorm_w, hgrn_w_out,
              swa_w_q, swa_sinks, swa_w_out, shared_w_kv, rel_bias,
              ffn_w_in, ffn_conv_w, ffn_conv_b, ffn_w_out,
              ln_mix_g, ln_mix_b, ln_ffn_g, ln_ffn_b):
    B, S, D = x.shape
    n_blocks = S // SW_WINDOW
    lower_bounds = jnp.cumsum(jax.nn.softmax(hgrn_lb_logits.astype(jnp.float32), axis=0), axis=0)
    bias, mask = banded_bias_and_mask(rel_bias, n_blocks)

    h = x
    k_shared = v_shared = None
    for layer in range(DEPTH):
        if layer < N_A_LAYERS_2:
            mix = hgrn2_mixer(h, hgrn_w_in[layer], lower_bounds[layer],
                              hgrn_gnorm_w[layer], hgrn_w_out[layer])
        else:
            j = layer - N_A_LAYERS_2
            mix = swa_sink_mixer(h, k_shared, v_shared, swa_w_q[j], swa_sinks[j],
                                 bias, mask, swa_w_out[j])
        h = layer_norm(ALPHA * h + mix, ln_mix_g[layer], ln_mix_b[layer])
        ff = conv_ffn(h, ffn_w_in[layer], ffn_conv_w[layer], ffn_conv_b[layer], ffn_w_out[layer])
        h = layer_norm(ALPHA * h + ff, ln_ffn_g[layer], ln_ffn_b[layer])
        if layer == N_A_LAYERS_2 - 1:
            k_flat, v_flat = jnp.split(h @ shared_w_kv, 2, axis=-1)
            k_shared = k_flat.reshape(B, S, SW_KV_HEADS, SW_HEAD_DIM)
            v_shared = v_flat.reshape(B, S, SW_KV_HEADS, SW_HEAD_DIM)
    return h


def setup_inputs(seed=0):
    out = dict(first_inputs(seed))
    for name, value in second_inputs(seed + 1).items():
        if name != "x":
            out[name + "_2"] = value
    return out


def reference(
    x, norm_mix, w_qkv_a, w_o_a, norm_kv, w_kv, w_q_b, w_o_b, norm_ffn, w_gate, w_up, w_down,
    norm_final, hgrn_w_in_2, hgrn_lb_logits_2, hgrn_gnorm_w_2, hgrn_w_out_2, swa_w_q_2,
    swa_sinks_2, swa_w_out_2, shared_w_kv_2, rel_bias_2, ffn_w_in_2, ffn_conv_w_2, ffn_conv_b_2,
    ffn_w_out_2, ln_mix_g_2, ln_mix_b_2, ln_ffn_g_2, ln_ffn_b_2,
):
    x = first_block(
        x, norm_mix, w_qkv_a, w_o_a, norm_kv, w_kv, w_q_b, w_o_b, norm_ffn, w_gate, w_up,
        w_down, norm_final,
    )
    return second_block(
        x, hgrn_w_in_2, hgrn_lb_logits_2, hgrn_gnorm_w_2, hgrn_w_out_2, swa_w_q_2, swa_sinks_2,
        swa_w_out_2, shared_w_kv_2, rel_bias_2, ffn_w_in_2, ffn_conv_w_2, ffn_conv_b_2,
        ffn_w_out_2, ln_mix_g_2, ln_mix_b_2, ln_ffn_g_2, ln_ffn_b_2,
    )


_drawn_inputs = setup_inputs


def setup_inputs(seed=0):
    import zlib

    import numpy as np

    out = dict(_drawn_inputs(seed))
    spreads = {}
    factors = {'norm_mix': 3.402,
     'norm_kv': 8.0,
     'norm_ffn': 3.038,
     'norm_final': 2.821,
     'hgrn_lb_logits_2': 4.947,
     'hgrn_gnorm_w_2': 29.438,
     'swa_sinks_2': 31.274,
     'rel_bias_2': 4.545,
     'ffn_conv_b_2': 8.0}
    for name, (base, spread) in spreads.items():
        noise = np.random.default_rng([zlib.crc32(name.encode()), seed]).standard_normal(out[name].shape)
        drawn = base * np.exp(spread * noise) if base else spread * noise
        out[name] = __import__('jax').numpy.asarray(drawn.astype(out[name].dtype))
    for name, factor in factors.items():
        out[name] = (out[name] * factor).astype(out[name].dtype)
    return out
```

```python
from contextlib import ExitStack

import numpy as np

import concourse.bass as bass
from concourse import mybir

F32 = mybir.dt.float32
F32R = mybir.dt.float32r
I32 = mybir.dt.int32
ALU = mybir.AluOpType
ACT = mybir.ActivationFunctionType

P = 128
S = 512
D = 1024
KT = D // P
SB = S // P
FF = 2816
FT = FF // P
HEADS = 16
HD = D // HEADS
PAIRS = HEADS // 2
HG = 8
WINDOW = 128
BUCKETS = 32
MAX_DIST = 128
SCALE = float(HD) ** -0.5
ALPHA = 4.0 ** 0.25
RMS_EPS = 1e-6
LN_EPS = 1e-5
NEG = -1.0e30

SLOTS = 3
SLAB = 1024

TRI = 1280
Q_AT = {3: 0, 2: 512, 0: 896, 1: 1024}
K_AT = {0: 0, 1: 512, 3: 896, 2: 1024}
WIN = 896
WQ_AT = {1: 0, 2: 256, 3: 512, 0: 768}
WK_AT = {0: 0, 1: 256, 2: 512, 3: 768}

VECTORS = ["mix0", "mix1", "kv", "ffn0", "ffn1", "final", "lb0", "lb1", "lnmg0", "lnmb0", "lnmg1",
           "lnmb1", "lnfg0", "lnfb0", "lnfg1", "lnfb1"]
VEC_AT = {name: KT * n for n, name in enumerate(VECTORS)}
GN_AT = KT * len(VECTORS)
VEC_COLS = GN_AT + 1
CONST_AT = {}
_at = 0
for _name, _w in (("ident", P), ("diagmask", P), ("rot", P), ("count", S), ("cos", S), ("sin", S)):
    CONST_AT[_name] = (_at, _w)
    _at += _w
CONST_COLS = _at
LEVELS = 8


class Phase:

    def __init__(self, name, iters, slots):
        self.name, self.iters, self.slots = name, iters, slots


HALF11 = [0, 1] * 5 + [2]
PHASES = [
    Phase("stick", PAIRS, [0, 1, 2]), Phase("stick_out", 2, [0, 1, 0, 1]),
    Phase("up0", FT // 2, [0, 1, 0, 1]), Phase("down0", 2, HALF11),
    Phase("dilated", PAIRS, [0, 1, 2]), Phase("dilated_out", 2, [0, 1, 0, 1]),
    Phase("up1", FT // 2, [0, 1, 0, 1]), Phase("down1", 2, HALF11),
    Phase("hgrn", HG, [0, 1, 0, 1]), Phase("hgrn_out", 2, [0, 1, 0, 1]),
    Phase("up2", FT // 2, [0, 1, 0, 1]), Phase("down2", 2, HALF11),
    Phase("window", PAIRS, [0, 1, 2]), Phase("window_out", 2, [0, 1, 0, 1]),
    Phase("up3", FT // 2, [0, 1, 0, 1]), Phase("down3", 2, HALF11),
]
_n, _seen = 0, [0] * SLOTS
for _p in PHASES:
    _p.first, _p.seen = _n, list(_seen)
    _n += _p.iters * len(_p.slots)
    for _s in _p.slots:
        _seen[_s] += _p.iters
TOTAL_SLABS = _n
PH = {p.name: p for p in PHASES}


def following(ph, i, k):
    per = len(ph.slots)
    if k >= per:
        if not isinstance(i, int) or i + 1 < ph.iters:
            return following(ph, i + 1, k - per)
        nxt = PHASES.index(ph) + 1
        if nxt == len(PHASES):
            return None
        return following(PHASES[nxt], 0, k - per)
    slot = ph.slots[k]
    each = ph.slots.count(slot)
    return ph.first + i * per + k, slot, ph.seen[slot] + i * each + ph.slots[:k + 1].count(slot)


def program(nc, x_t, weights, vectors, conv, consts, levels, resets, sinks, buckets, onehot, out_t):
    with ExitStack() as ctx:
        def sb(name, shape, dt=F32):
            return ctx.enter_context(nc.sbuf_tensor(name, shape, dt))

        def sem(name):
            return ctx.enter_context(nc.semaphore(name))

        hT = sb("hT", [P, KT, S])
        xh = sb("xh", [P, KT, S], F32R)
        xl = sb("xl", [P, KT, S], F32R)
        raw = [sb(f"raw{k}", [P, SLAB]) for k in range(SLOTS)]
        wh = [sb(f"wh{k}", [P, SLAB], F32R) for k in range(SLOTS)]
        wl = [sb(f"wl{k}", [P, SLAB], F32R) for k in range(SLOTS)]
        vec = sb("vec", [P, VEC_COLS])
        cst = sb("cst", [P, CONST_COLS])
        cvt = sb("cvt", [P, 2, 2 * FT, 4])
        ones = sb("ones", [P, P])
        small = sb("small", [P, 8])
        tiny = sb("tiny", [P, 16])
        identr = sb("identr", [P, P], F32R)
        maskr = sb("maskr", [P, P], F32R)
        rstd = sb("rstd", [P, S])
        acc = sb("acc", [P, S])
        lbs = sb("lbs", [P, 2, KT])
        base = nc.sbuf_base + (-nc.sbuf_base) % 32
        room = nc.sbuf_usable_end - base

        class Arena:

            def __init__(self, stage):
                self.stage, self.at = stage, 0

            def __call__(self, name, shape, dt=F32):
                n = 4
                for w in shape[1:]:
                    n *= w
                assert self.at + n <= room, (self.stage, name, self.at + n, room)
                t = nc.alloc_sbuf_tensor_at(f"{self.stage}_{name}", shape, dt, offset=base + self.at)
                self.at += n + (-n) % 32
                return t

        ps = ctx.enter_context(nc.psum_tensor("ps", [P, 8, S], F32))
        scratch = nc.dram_tensor("bias_rows", (HEADS, 3 * WINDOW), F32, kind="Internal").ap()

        def const(name):
            at, w = CONST_AT[name]
            return cst[:, at:at + w]

        def gain(name, j):
            return vec[:, VEC_AT[name] + j:VEC_AT[name] + j + 1]

        def w3(t, k):
            return t[:, k * P:(k + 1) * P]

        steps = []

        def step(dve):
            at = 1 + len(steps) % 15
            steps.append(at)
            dve.tensor_copy(tiny[:, at:at + 1], tiny[:, 0:1])

        signals = {}

        class Signal:

            def __init__(self, name, adds):
                if name not in signals:
                    signals[name] = [sem(name), 0]
                self.sem, self.before = signals[name]
                signals[name][1] += adds

            def __call__(self, n):
                return self.sem, n + self.before

        raw_ready = [sem(f"raw_ready{k}") for k in range(SLOTS)]
        hi_done, lo_done, w_used = sem("hi_done"), sem("lo_done"), sem("w_used")
        loaded = sem("loaded")
        x_in = sem("x_in")
        consts_made = sem("consts_made")
        ones_made = sem("ones_made")
        out_done = sem("out_done")

        block = ctx.enter_context(nc.Block())

        def fetch(sp, ph, i, k, wait=True):
            n, slot, _ = following(ph, i, k)
            if wait:
                sp.wait_ge(lo_done, n - 1)
            src = weights[n] if isinstance(n, int) else weights[bass.ds(n, 1)].rearrange("a p c -> (a p) c")
            sp.dma_start(raw[slot][:, :], src).then_inc(raw_ready[slot], 16)

        def split_hi(act, ph, i, k, wait=True):
            f = following(ph, i, k)
            if f is None:
                return
            n, slot, seen = f
            act.wait_ge(raw_ready[slot], seen * 16)
            if wait:
                act.wait_ge(w_used, n - 1)
            act.activation(wh[slot][:, :], raw[slot][:, :], ACT.Copy).then_inc(hi_done, 1)

        def split_lo(dve, ph, i, k):
            f = following(ph, i, k)
            if f is None:
                return
            n, slot, _ = f
            dve.wait_ge(hi_done, n + 1)
            dve.tensor_tensor(wl[slot][:, :], raw[slot][:, :], wh[slot][:, :].bitcast(F32),
                              ALU.subtract).then_inc(lo_done, 1)

        def products(pe, out, w_hi, w_lo, m_hi, m_lo, first, last, **kw):
            pe.matmul(out, w_hi, m_hi, start=first, stop=False, **kw)
            pe.matmul(out, w_hi, m_lo, start=False, stop=False, **kw)
            return pe.matmul(out, w_lo, m_hi, start=False, stop=last, **kw)

        def project(pe, ph, i, k, out, mh, ml, x_ready=None, between=None):
            n, slot, _ = following(ph, i, k)
            pe.wait_ge(lo_done, n + 1)
            for t in range(KT):
                if x_ready is not None:
                    pe.wait_ge(x_ready[0], x_ready[1] + t + 1)
                mm = products(pe, out, w3(wh[slot], t), w3(wl[slot], t), mh[:, t, :], ml[:, t, :],
                              t == 0, t == KT - 1)
                if t == KT - 1:
                    mm.then_inc(w_used, 1)
                elif between is not None:
                    between(t)
            if between is not None:
                between(KT - 1)

        class Out:

            def __init__(self, ph, mh, ml):
                self.ph, self.mh, self.ml = ph, mh, ml
                self.tile_sum = Signal("tile_sum", KT - 2)
                self.h_ready = Signal("h_ready", KT)
                self.slabs = len(ph.slots)
                self.rounds = (self.slabs - 3) // 2 if self.slabs > 4 else 0

            def tile_done(self, n):
                half, jj = divmod(n - 1, 4)
                if jj < 3:
                    return self.tile_sum(3 * half + jj + 1)
                return w_used, self.ph.first + (half + 1) * self.slabs

            def pe(self, pe, ready):
                ph = self.ph

                def slab(half, k, i_expr=None):
                    c = k if i_expr is None else 2 * i_expr + k
                    n = ph.first + half * self.slabs + c
                    slot = ph.slots[k]
                    pe.wait_ge(lo_done, n + 1)
                    for jj in range(4):
                        bank = ps[:, half * 4 + jj, :]
                        for t in range(2):
                            if i_expr is None:
                                m_hi, m_lo = self.mh[:, 2 * k + t, :], self.ml[:, 2 * k + t, :]
                            else:
                                at = bass.ds(4 * i_expr + (2 * k + t), 1)
                                m_hi = self.mh[:, at, :].rearrange("p a s -> p (a s)")
                                m_lo = self.ml[:, at, :].rearrange("p a s -> p (a s)")
                            w = slice((t * 4 + jj) * P, (t * 4 + jj + 1) * P)
                            first = i_expr is None and k == 0 and t == 0
                            last = i_expr is None and k == self.slabs - 1 and t == 1
                            mm = products(pe, bank, wh[slot][:, w], wl[slot][:, w], m_hi, m_lo, first, last)
                            if last and jj < 3:
                                mm.then_inc(self.tile_sum.sem, 1)
                    mm.then_inc(w_used, 1)

                ready(pe)
                for half in range(2):
                    if self.rounds:
                        slab(half, 0)
                        slab(half, 1)
                        with pe.Fori(1, self.rounds) as c:
                            slab(half, 0, c)
                            slab(half, 1, c)
                    for k in range(2 * self.rounds, self.slabs):
                        slab(half, k)

            def splits(self, split, eng, half):
                ph = self.ph
                if self.rounds:
                    with eng.Fori(0, self.rounds) as c:
                        for k in range(2):
                            self.loop_split(split, eng, half, c, k)
                for k in range(2 * self.rounds, self.slabs):
                    split(eng, ph, half, k + 2)

            def loop_split(self, split, eng, half, c, k):
                n0, slot, seen0 = following(self.ph, half, k + 2)
                if split is split_hi:
                    eng.wait_ge(raw_ready[slot], (c + seen0) * 16)
                    eng.wait_ge(w_used, 2 * c + (n0 - 1))
                    eng.activation(wh[slot][:, :], raw[slot][:, :], ACT.Copy).then_inc(hi_done, 1)
                else:
                    eng.wait_ge(hi_done, 2 * c + (n0 + 1))
                    eng.tensor_tensor(wl[slot][:, :], raw[slot][:, :], wh[slot][:, :].bitcast(F32),
                                      ALU.subtract).then_inc(lo_done, 1)

            def fetches(self, sp):
                ph = self.ph
                for half in range(2):
                    if self.rounds:
                        with sp.Fori(0, self.rounds) as c:
                            for k in range(2):
                                n0, slot, _ = following(ph, half, k)
                                sp.wait_ge(lo_done, 2 * c + (n0 - 1))
                                src = weights[bass.ds(2 * c + n0, 1)].rearrange("a p c -> (a p) c")
                                sp.dma_start(raw[slot][:, :], src).then_inc(raw_ready[slot], 16)
                    for k in range(2 * self.rounds, self.slabs):
                        fetch(sp, ph, half, k)

        class Rms:

            xh_done, x_ready, sq_done, acc_done = sem("rms_xh"), sem("rms_x"), sem("rms_sq"), sem("rms_acc")
            sum_done, root_done, rstd_ready = sem("rms_sum"), sem("rms_root"), sem("rms_rstd")

            def __init__(self, n, gains, source):
                self.n, self.gain, self.source = n, gains, source
                self.tiles = n * KT

        def h_wait(eng, source, j):
            if source is None:
                eng.wait_ge(x_in, 16 * (j + 1))
            else:
                eng.wait_ge(*source.h_ready(j + 1))

        def rms_act_x(act, r, js):
            for j in js:
                h_wait(act, r.source, j)
                act.activation(xh[:, j, :], hT[:, j, :], ACT.Copy, scale=gain(r.gain, j)).then_inc(r.xh_done, 1)

        def rms_act_sq(act, r, sq, js):
            for j in js:
                if j >= 2:
                    act.wait_ge(r.acc_done, r.tiles + j - 1)
                act.activation(sq[:, j % 2, :], hT[:, j, :], ACT.Square).then_inc(r.sq_done, 1)

        def rms_dve_x(dve, r, j):
            dve.wait_ge(r.xh_done, r.tiles + j + 1)
            dve.scalar_tensor_tensor(out=xl[:, j, :], in0=hT[:, j, :], scalar=gain(r.gain, j),
                                     in1=xh[:, j, :].bitcast(F32), op0=ALU.mult,
                                     op1=ALU.subtract).then_inc(r.x_ready, 1)

        def rms_dve_acc(dve, r, sq, js):
            for j in js:
                dve.wait_ge(r.sq_done, r.tiles + j + 1)
                if j:
                    dve.wait_ge(r.acc_done, r.tiles + j)
                    dve.tensor_tensor(acc[:, :], acc[:, :], sq[:, j % 2, :], ALU.add).then_inc(r.acc_done, 1)
                else:
                    dve.tensor_copy(acc[:, :], sq[:, 0, :]).then_inc(r.acc_done, 1)

        def rms_pe(pe, r, bank):
            pe.wait_ge(r.acc_done, r.tiles + KT)
            pe.matmul(ps[:, bank, :], ones[:, :], acc[:, :], start=True, stop=True).then_inc(r.sum_done, 1)

        def rms_act_root(act, r, bank, width, eps):
            act.wait_ge(r.sum_done, r.n + 1)
            act.activation(acc[:, :], ps[:, bank, :], ACT.Sqrt, scale=1.0 / width,
                           bias=small[:, eps:eps + 1]).then_inc(r.root_done, 1)

        def rms_dve_rstd(dve, r):
            dve.wait_ge(r.root_done, r.n + 1)
            dve.reciprocal(rstd[:, :], acc[:, :]).then_inc(r.rstd_ready, 1)

        def add_half(dve, o, half, scale=None, after=None):
            for jj in range(4):
                j = half * 4 + jj
                dve.wait_ge(*o.tile_done(j + 1))
                if scale is None:
                    dve.tensor_tensor(hT[:, j, :], hT[:, j, :], ps[:, j, :], ALU.add).then_inc(o.h_ready.sem, 1)
                else:
                    dve.scalar_tensor_tensor(out=hT[:, j, :], in0=hT[:, j, :], scalar=scale,
                                             in1=ps[:, j, :], op0=ALU.mult, op1=ALU.add).then_inc(o.h_ready.sem, 1)
                if after is not None and jj:
                    after(j - 1)
            if after is not None:
                after(half * 4 + 3)

        class Out_then_rms:

            def __init__(self, o, r, sq):
                self.o, self.r, self.sq = o, r, sq

            def act(self, act):
                for half in range(2):
                    self.o.splits(split_hi, act, half)
                    rms_act_x(act, self.r, range(half * 4, half * 4 + 4))
                    rms_act_sq(act, self.r, self.sq, range(half * 4, half * 4 + 4))

            def dve(self, dve):
                for half in range(2):
                    self.o.splits(split_lo, dve, half)
                    add_half(dve, self.o, half, after=lambda j: rms_dve_x(dve, self.r, j))
                    rms_dve_acc(dve, self.r, self.sq, range(half * 4, half * 4 + 4))

        class Layer:

            first_done, mean_sum, mean_ready = sem("ln_first"), sem("ln_mean_sum"), sem("ln_mean")
            centered, sq_done, acc_done = sem("ln_centered"), sem("ln_sq"), sem("ln_acc")
            sum_done, root_done, rstd_ready = sem("ln_sum"), sem("ln_root"), sem("ln_rstd")
            scaled, h_new, xh_done, x_ready = sem("ln_scaled"), sem("ln_h"), sem("ln_xh"), sem("ln_x")

            def __init__(self, n, g, b):
                self.n, self.g, self.b = n, g, b
                self.tiles = n * KT

        def layer_dve(dve, o, L, mu, sq):
            for half in range(2):
                o.splits(split_lo, dve, half)
                add_half(dve, o, half, scale=ALPHA)
                for jj in range(4):
                    j = half * 4 + jj
                    dve.wait_ge(*o.h_ready(j + 1))
                    if j:
                        dve.wait_ge(L.first_done, L.tiles + j)
                        dve.tensor_tensor(acc[:, :], acc[:, :], hT[:, j, :], ALU.add).then_inc(L.first_done, 1)
                    else:
                        dve.tensor_copy(acc[:, :], hT[:, 0, :]).then_inc(L.first_done, 1)
            dve.wait_ge(L.mean_ready, L.n + 1)
            for j in range(KT):
                dve.tensor_tensor(hT[:, j, :], hT[:, j, :], mu[:, :], ALU.subtract).then_inc(L.centered, 1)
                if j:
                    layer_sum(dve, L, sq, j - 1)
            layer_sum(dve, L, sq, KT - 1)
            rms_dve_rstd(dve, L)
            dve.wait_ge(L.rstd_ready, L.n + 1)
            for j in range(KT):
                dve.tensor_tensor(hT[:, j, :], hT[:, j, :], rstd[:, :], ALU.mult).then_inc(L.scaled, 1)
                if j:
                    layer_low(dve, L, j - 1)
            layer_low(dve, L, KT - 1)

        def layer_sum(dve, L, sq, j):
            dve.wait_ge(L.sq_done, L.tiles + j + 1)
            if j:
                dve.wait_ge(L.acc_done, L.tiles + j)
                dve.tensor_tensor(acc[:, :], acc[:, :], sq[:, j % 2, :], ALU.add).then_inc(L.acc_done, 1)
            else:
                dve.tensor_copy(acc[:, :], sq[:, 0, :]).then_inc(L.acc_done, 1)

        def layer_low(dve, L, j):
            dve.wait_ge(L.xh_done, L.tiles + j + 1)
            dve.tensor_tensor(xl[:, j, :], hT[:, j, :], xh[:, j, :].bitcast(F32),
                              ALU.subtract).then_inc(L.x_ready, 1)

        def layer_act(act, o, L, mu, sq):
            for half in range(2):
                o.splits(split_hi, act, half)
            act.wait_ge(L.mean_sum, L.n + 1)
            act.activation(mu[:, :], ps[:, 0, :], ACT.Copy, scale=1.0 / D).then_inc(L.mean_ready, 1)
            for j in range(KT):
                act.wait_ge(L.centered, L.tiles + j + 1)
                if j >= 2:
                    act.wait_ge(L.acc_done, L.tiles + j - 1)
                act.activation(sq[:, j % 2, :], hT[:, j, :], ACT.Square).then_inc(L.sq_done, 1)
            rms_act_root(act, L, 1, D, 1)
            for j in range(KT):
                act.wait_ge(L.scaled, L.tiles + j + 1)
                act.activation(hT[:, j, :], hT[:, j, :], ACT.Identity, scale=gain(L.g, j),
                               bias=gain(L.b, j)).then_inc(L.h_new, 1)
                act.wait_ge(L.h_new, L.tiles + j + 1)
                act.activation(xh[:, j, :], hT[:, j, :], ACT.Copy).then_inc(L.xh_done, 1)

        def layer_pe(pe, L):
            pe.wait_ge(L.first_done, L.tiles + KT)
            pe.matmul(ps[:, 0, :], ones[:, :], acc[:, :], start=True, stop=True).then_inc(L.mean_sum, 1)
            pe.wait_ge(L.acc_done, L.tiles + KT)
            pe.matmul(ps[:, 1, :], ones[:, :], acc[:, :], start=True, stop=True).then_inc(L.sum_done, 1)

        class Pairs:
            def __init__(self, kind, ph):
                self.kind, self.ph = kind, ph
                a = Arena(kind)
                self.oh, self.ol = a("oh", [P, KT, S], F32R), a("ol", [P, KT, S], F32R)
                if kind == "dilated":
                    self.x2h, self.x2l = a("x2h", [P, KT, S], F32R), a("x2l", [P, KT, S], F32R)
                    self.t1 = a("t1", [P, S])
                    self.x2h_done, self.x2_ready = sem("x2h"), sem("x2")
                self.qh, self.ql = a("qh", [P, S], F32R), a("ql", [P, S], F32R)
                self.kh, self.kl = a("kh", [P, S], F32R), a("kl", [P, S], F32R)
                self.qs, self.vs = a("qs", [P, S]), a("vs", [P, S])
                self.vh, self.vl = a("vh", [P, SB, 2, P], F32R), a("vl", [P, SB, 2, P], F32R)
                self.cols = WIN if kind == "window" else TRI
                self.pth, self.ptl = a("pth", [P, self.cols], F32R), a("ptl", [P, self.cols], F32R)
                if kind == "stick":
                    self.stay, self.brk = a("stay", [P, TRI]), a("brk", [P, TRI])
                    self.left, self.w = a("left", [P, TRI + 1]), a("w", [P, TRI])
                    self.resets = a("resets", [P, TRI])
                    self.prob = [self.w, self.w]
                else:
                    self.prob = [a("pA", [P, self.cols]), a("pB", [P, self.cols])]
                    self.negm, self.den, self.inv = a("negm", [P, 8]), a("den", [P, 8]), a("inv", [P, 8])
                if kind == "window":
                    self.bias = a("bias", [P, HEADS, 2 * WINDOW])
                    self.sink, self.negsink, self.esink = a("sink", [P, HEADS]), a("negsink", [P, HEADS]), a("esink", [P, 8])
                    self.bcur, self.scur = a("bcur", [P, 2, 2 * WINDOW]), a("scur", [P, 2, 2])
                if kind == "stick":
                    self.sq = a("sq", [P, 2, S])
                    self.table, self.one_hot, self.rows = (
                        a("table", [P, HEADS]), a("one_hot", [P, 3 * WINDOW]), a("rows", [P, 3 * WINDOW]))
                self.qs_ready, self.qh_ready = Signal("pair_qs_ready", PAIRS), Signal("pair_qh_ready", PAIRS)
                self.q_ready, self.ks_ready = Signal("pair_q_ready", PAIRS), Signal("pair_ks_ready", PAIRS)
                self.kh_ready, self.k_ready = Signal("pair_kh_ready", PAIRS), Signal("pair_k_ready", PAIRS)
                self.vs_ready, self.vT_done = Signal("pair_vs_ready", PAIRS), Signal("pair_vT_done", PAIRS)
                self.vh_ready, self.v_ready = Signal("pair_vh_ready", HEADS), Signal("pair_v_ready", PAIRS)
                self.z_done, self.p_ready = Signal("pair_z_done", HEADS), Signal("pair_p_ready", HEADS)
                self.pT_done, self.ph_ready = Signal("pair_pT_done", HEADS), Signal("pair_ph_ready", HEADS)
                self.pl_ready, self.pv_done = Signal("pair_pl_ready", HEADS), Signal("pair_pv_done", HEADS)
                self.oh_ready, self.o_ready = Signal("pair_oh_ready", PAIRS), Signal("pair_o_ready", PAIRS)
                self.padded = Signal("pair_padded", 2)
                if kind == "stick":
                    self.stay_ready, self.brk_ready = Signal("pair_stay_ready", HEADS), Signal("pair_brk_ready", HEADS)
                    self.scan_done = Signal("pair_scan_done", HEADS)
                else:
                    self.max_done, self.exp_done = Signal("pair_max_done", HEADS), Signal("pair_exp_done", HEADS)
                    self.inv_done = Signal("pair_inv_done", HEADS)
                if kind == "dilated":
                    self.rot_done, self.cos_done = Signal("pair_rot_done", HEADS), Signal("pair_cos_done", HEADS)
                    self.sin_done, self.rope_done = Signal("pair_sin_done", HEADS), Signal("pair_rope_done", HEADS)
                if kind == "window":
                    self.cur_ready, self.den_done = Signal("pair_cur_ready", 3 * PAIRS), Signal("pair_den_done", HEADS)
                    self.esink_done = Signal("pair_esink_done", HEADS)

        def q_cols(a, h):
            if a.kind == "window":
                return [(i, WQ_AT[i], (max(i - 1, 0) * P, (i + 1) * P)) for i in (1, 2, 3, 0)]
            return [(i, Q_AT[i], (0, (i + 1) * P)) for i in (3, 2, 0, 1)]

        def flat(b0, b1):
            return ps[:, b0:b1, :].rearrange("p b s -> p (b s)")

        def pe_scores(pe, a, j, hh):
            rows = slice(hh * HD, (hh + 1) * HD)
            if hh == 0:
                pe.wait_ge(*a.q_ready(j + 1))
                pe.wait_ge(*a.k_ready(j + 1))
            else:
                pe.wait_ge(*(a.brk_ready if a.kind == "stick" else a.max_done)(2 * j + 1))
            out = flat(0, 3)
            for i, at, (k0, k1) in q_cols(a, hh):
                o = out[:, at:at + k1 - k0]
                q = slice(i * P, (i + 1) * P)
                stick = a.kind == "stick"
                mm = products(pe, o, a.qh[rows, q], a.ql[rows, q], a.kh[rows, k0:k1], a.kl[rows, k0:k1],
                              True, not stick)
                if stick:
                    mm = pe.matmul(out[:, at + i * P:at + (i + 1) * P], identr[:, :], maskr[:, :],
                                   start=False, stop=True)
            mm.then_inc(a.z_done.sem, 1)

        def pe_turn(pe, a, j, hh):
            pe.wait_ge(*a.p_ready(2 * j + hh + 1))
            out = flat(3, 6)
            src = a.prob[hh]
            for kb in range(SB):
                if a.kind == "window":
                    blocks, at = range(kb, min(kb + 2, SB)), WK_AT[kb]
                else:
                    blocks, at = range(kb, SB), K_AT[kb]
                for i in blocks:
                    if a.kind == "window":
                        c = WQ_AT[i] + (kb - max(i - 1, 0)) * P
                    else:
                        c = Q_AT[i] + kb * P
                    mm = pe.transpose(out[:, at + (i - kb) * P:at + (i - kb + 1) * P], src[:, c:c + P],
                                      const("ident"))
            mm.then_inc(a.pT_done.sem, 1)

        def pe_values(pe, a, j, hh):
            pe.wait_ge(*a.pl_ready(2 * j + hh + 1))
            if hh == 0:
                pe.wait_ge(*a.v_ready(j + 1))
            for kb in range(SB):
                if a.kind == "window":
                    at, n = WK_AT[kb], min(2, SB - kb) * P
                else:
                    at, n = K_AT[kb], (SB - kb) * P
                mm = products(pe, ps[:, 6, kb * P:kb * P + n], a.vh[:, kb, hh, :], a.vl[:, kb, hh, :],
                              a.pth[:, at:at + n], a.ptl[:, at:at + n], hh == 0 and kb == 0,
                              hh == 1 and kb == SB - 1, skip_group_check=True)
            mm.then_inc(a.pv_done.sem, 1)

        def pe_pair(pe, a, i, attn, proj, x_ready=None, stats=None):
            ph, j = a.ph, i - 1
            kvh, kvl = (a.x2h, a.x2l) if a.kind == "dilated" else (xh, xl)
            if attn:
                pe_scores(pe, a, j, 0)
            if proj:
                if attn:
                    pe.wait_ge(*a.v_ready(i))
                project(pe, ph, i, 0, ps[:, 7 if attn else 0, :], xh, xl, x_ready=x_ready)
            if stats is not None:
                stats()
            if attn:
                pe_scores(pe, a, j, 1)
            if proj:
                if a.kind == "dilated":
                    pe.wait_ge(*a.qs_ready(i + 1))
                    pe.matmul(ps[:, 6, :], const("rot"), a.qs[:, :], start=True, stop=True).then_inc(a.rot_done.sem, 1)
            if attn:
                pe_turn(pe, a, j, 0)
            if proj:
                pe.wait_ge(*a.qs_ready(i + 1))
                project(pe, ph, i, 1, ps[:, 7, :], kvh, kvl,
                        x_ready=(a.x2_ready, 0) if a.kind == "dilated" and not attn else None)
            if attn:
                if proj and a.kind == "dilated":
                    pe.wait_ge(*a.sin_done(2 * i + 1))
                pe_values(pe, a, j, 0)
            if proj and a.kind == "dilated":
                pe.wait_ge(*a.ks_ready(i + 1))
                pe.matmul(ps[:, 7, :], const("rot"), a.qs[:, :], start=True, stop=True).then_inc(a.rot_done.sem, 1)
            if attn:
                pe_turn(pe, a, j, 1)
            if proj:
                if a.kind == "dilated":
                    pe.wait_ge(*a.sin_done(2 * i + 2))
                else:
                    pe.wait_ge(*a.ks_ready(i + 1))
                project(pe, ph, i, 2, ps[:, 7, :], kvh, kvl)
            if attn:
                pe_values(pe, a, j, 1)
            if proj:
                pe.wait_ge(*a.vs_ready(i + 1))
                for b in range(SB):
                    mm = pe.transpose(ps[:, 7, b * P:(b + 1) * P], a.vs[:, b * P:(b + 1) * P], const("ident"))
                mm.then_inc(a.vT_done.sem, 1)

        def act_weights(act, a, j, hh):
            out = flat(0, 3)
            h = 2 * j + hh
            if a.kind == "stick":
                act.wait_ge(*a.z_done(h + 1))
                if hh == 1:
                    act.wait_ge(*a.p_ready(h))
                act.activation(a.stay[:, :], out[:, 0:TRI], ACT.Sigmoid, scale=-1.0).then_inc(a.stay_ready.sem, 1)
                act.activation(a.brk[:, :], out[:, 0:TRI], ACT.Sigmoid).then_inc(a.brk_ready.sem, 1)
                return
            p = a.prob[hh]
            act.wait_ge(*a.max_done(h + 1))
            for n, (i, at, (k0, k1)) in enumerate(q_cols(a, hh)):
                c = 4 * hh + n
                e = act.activation(p[:, at:at + k1 - k0], p[:, at:at + k1 - k0], ACT.Exp, scale=-1.0,
                                   bias=a.negm[:, c:c + 1], accum_out=a.den[:, c:c + 1])
            e.then_inc(a.exp_done.sem, 1)
            if a.kind == "window":
                act.activation(a.esink[:, 4 * hh:4 * hh + 4], a.negm[:, 4 * hh:4 * hh + 4], ACT.Exp,
                               bias=a.scur[:, 0, hh:hh + 1]).then_inc(a.esink_done.sem, 1)

        def act_pT(act, a, j, hh):
            act.wait_ge(*a.pT_done(2 * j + hh + 1))
            if hh == 1:
                act.wait_ge(*a.pv_done(2 * j + 1))
            act.activation(a.pth[:, :], flat(3, 6)[:, 0:a.cols], ACT.Copy).then_inc(a.ph_ready.sem, 1)

        def backwards(ap):
            return ap.rearrange("p (b q) -> p b q", b=SB)[:, :, ::-1]

        def forwards(ap):
            return ap.rearrange("p (b q) -> p b q", b=SB)

        def act_pair(act, a, i, attn, proj):
            ph, j = a.ph, i - 1
            if attn:
                act_weights(act, a, j, 0)
            if proj:
                split_hi(act, ph, i, 2)
            if attn:
                act_weights(act, a, j, 1)
            if proj:
                if a.kind == "dilated":
                    act.wait_ge(*a.rope_done(2 * i + 1))
                else:
                    act.wait_ge(*a.qs_ready(i + 1))
                if attn:
                    act.wait_ge(*a.z_done(2 * i))
                if a.kind == "window":
                    act.activation(backwards(a.qh[:, :]), forwards(a.qs[:, :]), ACT.Copy, scale=SCALE)\
                       .then_inc(a.qh_ready.sem, 1)
                else:
                    src = a.t1 if a.kind == "dilated" else a.qs
                    act.activation(a.qh[:, :], src[:, :], ACT.Copy, scale=SCALE).then_inc(a.qh_ready.sem, 1)
            if attn:
                act_pT(act, a, j, 0)
            if proj:
                split_hi(act, ph, i, 3)
                if a.kind == "dilated":
                    act.wait_ge(*a.rope_done(2 * i + 2))
                else:
                    act.wait_ge(*a.ks_ready(i + 1))
                src = a.t1 if a.kind == "dilated" else a.qs
                act.activation(a.kh[:, :], src[:, :], ACT.Copy).then_inc(a.kh_ready.sem, 1)
            if attn:
                act_pT(act, a, j, 1)
            if proj:
                split_hi(act, ph, i, 4)
                act.wait_ge(*a.vT_done(i + 1))
                for v in range(2):
                    vT = ps[:, 7, :].rearrange("p (b d) -> p b d", b=SB)[:, :, v * HD:(v + 1) * HD]
                    act.activation(a.vh[:, :, v, v * HD:(v + 1) * HD], vT, ACT.Copy).then_inc(a.vh_ready.sem, 1)

        def dve_weights(dve, a, j, hh):
            h = 2 * j + hh
            if a.kind == "stick":
                dve.wait_ge(*a.stay_ready(h + 1))
                dve.tensor_tensor_scan(a.left[:, 0:TRI][:, ::-1],
                                       a.stay[:, ::-1], a.resets[:, ::-1], 1.0, ALU.mult,
                                       ALU.max).then_inc(a.scan_done.sem, 1)
                dve.wait_ge(*a.scan_done(h + 1))
                dve.wait_ge(*a.brk_ready(h + 1))
                if hh == 1:
                    dve.wait_ge(*a.pT_done(h))
                dve.tensor_tensor(a.w[:, :], a.brk[:, :], a.left[:, 1:TRI + 1], ALU.mult).then_inc(a.p_ready.sem, 1)
                return
            out = flat(0, 3)
            dve.wait_ge(*a.z_done(h + 1))
            if a.kind == "window":
                dve.wait_ge(*a.cur_ready(3 * j + 3))
            step(dve)
            for n, (i, at, (k0, k1)) in enumerate(q_cols(a, hh)):
                w = k1 - k0
                c = 4 * hh + n
                if a.kind == "window":
                    add = a.bcur[:, hh, 2 * WINDOW - w:2 * WINDOW]
                    start = a.scur[:, 1, hh:hh + 1]
                else:
                    add = const("count")[:, (SB - 1 - i) * P:S]
                    start = 3.0e38
                m = dve.tensor_tensor_reduce(out=a.prob[hh][:, at:at + w], in0=out[:, at:at + w], in1=add,
                                             scale=-1.0, scalar=start, op0=ALU.add, op1=ALU.min,
                                             accum_out=a.negm[:, c:c + 1])
            m.then_inc(a.max_done.sem, 1)

        def dve_scale(dve, a, j, hh):
            if a.kind == "stick":
                return
            h = 2 * j + hh
            cs = slice(4 * hh, 4 * hh + 4)
            dve.wait_ge(*a.exp_done(h + 1))
            if a.kind == "window":
                dve.wait_ge(*a.esink_done(h + 1))
                dve.tensor_tensor(a.den[:, cs], a.den[:, cs], a.esink[:, cs], ALU.add).then_inc(a.den_done.sem, 1)
                dve.wait_ge(*a.den_done(h + 1))
            dve.reciprocal(a.inv[:, cs], a.den[:, cs]).then_inc(a.inv_done.sem, 1)
            dve.wait_ge(*a.inv_done(h + 1))
            for n, (i, at, (k0, k1)) in enumerate(q_cols(a, hh)):
                p = a.prob[hh][:, at:at + k1 - k0]
                s = dve.tensor_scalar(p, p, a.inv[:, 4 * hh + n:4 * hh + n + 1], None, ALU.mult)
            s.then_inc(a.p_ready.sem, 1)

        def dve_pT(dve, a, j, hh):
            dve.wait_ge(*a.ph_ready(2 * j + hh + 1))
            dve.tensor_tensor(a.ptl[:, :], flat(3, 6)[:, 0:a.cols], a.pth[:, :].bitcast(F32),
                              ALU.subtract).then_inc(a.pl_ready.sem, 1)

        def dve_rope(dve, a, i, which):
            bank = 6 if which == 0 else 7
            dve.wait_ge(*a.rot_done(2 * i + which + 1))
            dve.wait_ge(*a.cos_done(2 * i + which + 1))
            dve.tensor_tensor(a.qs[:, :], ps[:, bank, :], const("sin"), ALU.mult).then_inc(a.sin_done.sem, 1)
            dve.wait_ge(*a.sin_done(2 * i + which + 1))
            dve.tensor_tensor(a.t1[:, :], a.t1[:, :], a.qs[:, :], ALU.add).then_inc(a.rope_done.sem, 1)

        def dve_pair(dve, a, i, attn, proj):
            ph, j = a.ph, i - 1
            if attn:
                if a.kind == "window":
                    at = bass.ds(2 * j, 2)
                    dve.tensor_scalar(a.bcur[:, :, :], a.bias[:, at, :], 1.0, None, ALU.mult).then_inc(a.cur_ready.sem, 1)
                    dve.tensor_scalar(a.scur[:, 0, :], a.sink[:, at], 1.0, None, ALU.mult).then_inc(a.cur_ready.sem, 1)
                    dve.tensor_scalar(a.scur[:, 1, :], a.negsink[:, at], 1.0, None, ALU.mult).then_inc(a.cur_ready.sem, 1)
                dve_weights(dve, a, j, 0)
                dve_scale(dve, a, j, 0)
            if proj:
                dve.wait_ge(w_used, ph.first + 3 * i + 1)
                take(dve, a, a.qs, 7 if attn else 0).then_inc(a.qs_ready.sem, 1)
                split_lo(dve, ph, i, 2)
            if attn and a.kind != "stick":
                dve_weights(dve, a, j, 1)
            if proj:
                if a.kind == "dilated":
                    dve_rope(dve, a, i, 0)
                    dve.wait_ge(*a.rope_done(2 * i + 1))
                src = a.t1 if a.kind == "dilated" else a.qs
                dve.wait_ge(*a.qh_ready(i + 1))
                o, s, h = a.ql[:, :], src[:, :], a.qh[:, :].bitcast(F32)
                if a.kind == "window":
                    o, s, h = backwards(o), forwards(s), backwards(h)
                dve.scalar_tensor_tensor(out=o, in0=s, scalar=SCALE, in1=h, op0=ALU.mult,
                                         op1=ALU.subtract).then_inc(a.q_ready.sem, 1)
            if attn:
                dve_pT(dve, a, j, 0)
                if a.kind == "stick":
                    dve_weights(dve, a, j, 1)
                dve_scale(dve, a, j, 1)
            if proj:
                dve.wait_ge(w_used, ph.first + 3 * i + 2)
                dve.wait_ge(*a.q_ready(i + 1))
                take(dve, a, a.qs).then_inc(a.ks_ready.sem, 1)
                split_lo(dve, ph, i, 3)
                if a.kind == "dilated":
                    dve_rope(dve, a, i, 1)
                    dve.wait_ge(*a.rope_done(2 * i + 2))
                src = a.t1 if a.kind == "dilated" else a.qs
                dve.wait_ge(*a.kh_ready(i + 1))
                dve.wait_ge(*a.ks_ready(i + 1))
                dve.tensor_tensor(a.kl[:, :], src[:, :], a.kh[:, :].bitcast(F32), ALU.subtract).then_inc(a.k_ready.sem, 1)
            if attn:
                dve_pT(dve, a, j, 1)
            if proj:
                dve.wait_ge(w_used, ph.first + 3 * i + 3)
                take(dve, a, a.vs).then_inc(a.vs_ready.sem, 1)
                split_lo(dve, ph, i, 4)
            if attn:
                dve.wait_ge(*a.pv_done(2 * j + 2))
                at = bass.ds(j, 1) if not isinstance(j, int) else slice(j, j + 1)
                oh = a.oh[:, at, :].rearrange("p a s -> p (a s)")
                ol = a.ol[:, at, :].rearrange("p a s -> p (a s)")
                src = ps[:, 6, :]
                if a.kind == "window":
                    oh, ol, src = forwards(oh), forwards(ol), backwards(src)
                dve.tensor_scalar(oh, src, 1.0, None, ALU.mult).then_inc(a.oh_ready.sem, 1)
                dve.wait_ge(*a.oh_ready(j + 1))
                dve.tensor_tensor(ol, src, oh.bitcast(F32), ALU.subtract).then_inc(a.o_ready.sem, 1)
            if proj:
                dve.wait_ge(*a.vh_ready(2 * i + 2))
                for v in range(2):
                    vT = ps[:, 7, :].rearrange("p (b d) -> p b d", b=SB)[:, :, v * HD:(v + 1) * HD]
                    cols = slice(v * HD, (v + 1) * HD)
                    m = dve.tensor_tensor(a.vl[:, :, v, cols], vT, a.vh[:, :, v, cols].bitcast(F32), ALU.subtract)
                m.then_inc(a.v_ready.sem, 1)

        def take(dve, a, dst, bank=7):
            if a.kind == "window":
                return dve.tensor_scalar(dst[:, :], ps[:, bank, :], 1.0, None, ALU.mult)
            return dve.tensor_tensor(dst[:, :], ps[:, bank, :], rstd[:, :], ALU.mult)

        def pool_pair(pool, a, i):
            for which, ready in ((0, a.qs_ready), (1, a.ks_ready)):
                pool.wait_ge(*ready(i + 1))
                if which == 0:
                    if not isinstance(i, int) or i:
                        pool.wait_ge(*a.k_ready(i))
                else:
                    pool.wait_ge(*a.q_ready(i + 1))
                pool.tensor_tensor(a.t1[:, :], a.qs[:, :], const("cos"), ALU.mult).then_inc(a.cos_done.sem, 1)

        class Up:
            def __init__(self, name, ph, conv_layer=None):
                self.ph, self.conv = ph, conv_layer
                a = Arena(name)
                self.ah, self.al = a("ah", [P, FT, S], F32R), a("al", [P, FT, S], F32R)
                self.g, self.s, self.u = a("g", [P, S]), a("s", [P, S]), a("u", [P, S])
                self.sq = a("sq", [P, 2, S])
                self.cur = a("cur", [P, 2, 4])
                self.mu = self.g
                self.s_ready, self.pr_ready = Signal("up_s_ready", FT), Signal("up_pr_ready", FT)
                self.ah_ready, self.a_ready = Signal("up_ah_ready", FT), Signal("up_a_ready", FT)
                if conv_layer is None:
                    self.g_ready, self.u_ready = Signal("up_g_ready", FT), Signal("up_u_ready", FT)
                else:
                    self.cur_ready, self.y_ready = Signal("up_cur_ready", FT), Signal("up_y_ready", 2 * FT)
                    self.c1_done, self.c2_done = Signal("up_c1_done", 2 * FT), Signal("up_c2_done", 2 * FT)

        def up_pe(pe, u, r, stats):
            ph = u.ph

            def tile(i, par, first=False):
                for k in range(2):
                    if not first:
                        pe.wait_ge(*u.a_ready(2 * i + par - 1))
                    project(pe, ph, i, 2 * par + k, ps[:, 2 * par + k, :], xh, xl,
                            x_ready=(r.x_ready, r.tiles) if first and par == 0 and k == 0 else None)
                    if first and par == 0 and k == 0 and stats is not None:
                        stats()

            tile(0, 0, True)
            tile(0, 1, True)
            with pe.Fori(1, FT // 2) as i:
                tile(i, 0)
                tile(i, 1)

        def up_act(act, u):
            ph = u.ph

            def tile(i, par):
                t = 2 * i + par
                bg, bu = ps[:, 2 * par, :], ps[:, 2 * par + 1, :]
                if u.conv is None:
                    split_hi(act, ph, i, 2 * par + 2)
                    act.wait_ge(*u.g_ready(t + 1))
                    act.activation(u.s[:, :], u.g[:, :], ACT.Silu).then_inc(u.s_ready.sem, 1)
                    split_hi(act, ph, i, 2 * par + 3)
                else:
                    act.wait_ge(w_used, ph.first + 4 * i + 2 * par + 1)
                    act.wait_ge(*u.cur_ready(t + 1))
                    act.activation(u.g[:, :], bg, ACT.Identity, scale=u.cur[:, 0, 2:3],
                                   bias=u.cur[:, 0, 3:4]).then_inc(u.y_ready.sem, 1)
                    split_hi(act, ph, i, 2 * par + 2)
                    act.wait_ge(w_used, ph.first + 4 * i + 2 * par + 2)
                    act.activation(u.u[:, :], bu, ACT.Identity, scale=u.cur[:, 1, 2:3],
                                   bias=u.cur[:, 1, 3:4]).then_inc(u.y_ready.sem, 1)
                    split_hi(act, ph, i, 2 * par + 3)
                    act.wait_ge(*u.c2_done(2 * t + 1))
                    act.activation(u.s[:, :], u.g[:, :], ACT.Silu).then_inc(u.s_ready.sem, 1)

            with act.Fori(0, FT // 2 - 1) as i:
                tile(i, 0)
                tile(i, 1)
            tile(FT // 2 - 1, 0)
            tile(FT // 2 - 1, 1)

        def up_dve(dve, u):
            ph = u.ph

            def tap(t, which, y, bank, k):
                shift = 2 - k
                done = u.c1_done if k == 1 else u.c2_done
                if k == 1:
                    dve.wait_ge(*u.y_ready(2 * t + which + 1))
                else:
                    dve.wait_ge(*u.c1_done(2 * t + which + 1))
                dve.scalar_tensor_tensor(out=y[:, shift:S], in0=bank[:, 0:S - shift],
                                         scalar=u.cur[:, which, k:k + 1], in1=y[:, shift:S],
                                         op0=ALU.mult, op1=ALU.add).then_inc(done.sem, 1)

            def tile(i, par):
                t = 2 * i + par
                bg, bu = ps[:, 2 * par, :], ps[:, 2 * par + 1, :]
                at = bass.ds(t, 1) if not isinstance(t, int) else slice(t, t + 1)
                if u.conv is None:
                    dve.wait_ge(w_used, ph.first + 4 * i + 2 * par + 1)
                    dve.tensor_tensor(u.g[:, :], bg, rstd[:, :], ALU.mult).then_inc(u.g_ready.sem, 1)
                    split_lo(dve, ph, i, 2 * par + 2)
                    dve.wait_ge(w_used, ph.first + 4 * i + 2 * par + 2)
                    dve.tensor_tensor(u.u[:, :], bu, rstd[:, :], ALU.mult).then_inc(u.u_ready.sem, 1)
                    split_lo(dve, ph, i, 2 * par + 3)
                    dve.wait_ge(*u.s_ready(t + 1))
                    dve.wait_ge(*u.u_ready(t + 1))
                else:
                    src = cvt[:, u.conv, :, :].rearrange("p (w t) c -> p w t c", w=2)[:, :, at, :]
                    dve.tensor_scalar(u.cur[:, :, :], src.rearrange("p w t c -> p w (t c)"), 1.0, None,
                                      ALU.mult).then_inc(u.cur_ready.sem, 1)
                    dve.wait_ge(*u.cur_ready(t + 1))
                    tap(t, 0, u.g, bg, 1)
                    tap(t, 0, u.g, bg, 0)
                    split_lo(dve, ph, i, 2 * par + 2)
                    tap(t, 1, u.u, bu, 1)
                    tap(t, 1, u.u, bu, 0)
                    split_lo(dve, ph, i, 2 * par + 3)
                    dve.wait_ge(*u.c2_done(2 * t + 2))
                    dve.wait_ge(*u.s_ready(t + 1))
                dve.tensor_tensor(u.s[:, :], u.s[:, :], u.u[:, :], ALU.mult).then_inc(u.pr_ready.sem, 1)
                dve.wait_ge(*u.pr_ready(t + 1))
                oh = u.ah[:, at, :].rearrange("p a s -> p (a s)")
                ol = u.al[:, at, :].rearrange("p a s -> p (a s)")
                dve.tensor_scalar(oh, u.s[:, :], 1.0, None, ALU.mult).then_inc(u.ah_ready.sem, 1)
                dve.wait_ge(*u.ah_ready(t + 1))
                dve.tensor_tensor(ol, u.s[:, :], oh.bitcast(F32), ALU.subtract).then_inc(u.a_ready.sem, 1)

            with dve.Fori(0, FT // 2 - 1) as i:
                tile(i, 0)
                tile(i, 1)
            tile(FT // 2 - 1, 0)
            tile(FT // 2 - 1, 1)

        class Hgrn:

            def __init__(self, ph):
                self.ph = ph
                a = Arena("hgrn")
                self.oh, self.ol = a("oh", [P, KT, S], F32R), a("ol", [P, KT, S], F32R)
                self.F, self.Q, self.G, self.vs, self.sig = (a(n, [P, S]) for n in ("F", "Q", "G", "vs", "sig"))
                self.QF, self.KG, self.T = a("QF", [P, S]), a("KG", [P, S]), a("T", [P, S])
                self.qh = [a(f"qh{p}", [P, S], F32R) for p in range(2)]
                self.ql = [a(f"ql{p}", [P, S], F32R) for p in range(2)]
                self.kh = [a(f"kh{p}", [P, S], F32R) for p in range(2)]
                self.kl = [a(f"kl{p}", [P, S], F32R) for p in range(2)]
                self.sd, self.sdh, self.sdl = a("sd", [P, SB, P]), a("sdh", [P, SB, P], F32R), a("sdl", [P, SB, P], F32R)
                self.fh, self.fl = a("fh", [P, 768], F32R), a("fl", [P, 768], F32R)
                self.vh, self.vl = a("vh", [P, S], F32R), a("vl", [P, S], F32R)
                self.sq, self.root, self.rs, self.og = (a(n, [P, S]) for n in ("sq", "root", "rs", "og"))
                self.mask = a("mask", [P, LEVELS, P], I32)
                self.start_ready, self.hi_ready = sem("hgrn_start_ready"), sem("hgrn_hi_ready")
                self.lo_ready, self.uq_done = sem("hgrn_lo_ready"), sem("hgrn_uq_done")
                self.uk_done, self.ut_done = sem("hgrn_uk_done"), sem("hgrn_ut_done")
                self.prod_done, self.picked = sem("hgrn_prod_done"), sem("hgrn_picked")
                self.sdh_ready, self.sdl_ready = sem("hgrn_sdh_ready"), sem("hgrn_sdl_ready")
                self.fh_ready, self.fl_ready = sem("hgrn_fh_ready"), sem("hgrn_fl_ready")
                self.pv_done, self.sq_ready = sem("hgrn_pv_done"), sem("hgrn_sq_ready")
                self.sum_done, self.root_ready = sem("hgrn_sum_done"), sem("hgrn_root_ready")
                self.rs_ready, self.og_ready = sem("hgrn_rs_ready"), sem("hgrn_og_ready")
                self.gated, self.oh_ready = sem("hgrn_gated"), sem("hgrn_oh_ready")
                self.o_ready, self.sigf_ready = sem("hgrn_o_ready"), sem("hgrn_sigf_ready")
                self.F_ready, self.sigq_ready = sem("hgrn_F_ready"), sem("hgrn_sigq_ready")
                self.Q_ready, self.vs_ready = sem("hgrn_Q_ready"), sem("hgrn_vs_ready")
                self.vT_done, self.vh_ready = sem("hgrn_vT_done"), sem("hgrn_vh_ready")
                self.v_ready, self.sigg_ready = sem("hgrn_v_ready"), sem("hgrn_sigg_ready")
                self.G_ready, self.cleared = sem("hgrn_G_ready"), sem("hgrn_cleared")
                self.masks_in, self.lb_diff = sem("hgrn_masks_in"), sem("hgrn_lb_diff")
                self.lb_ready = sem("hgrn_lb_ready")

        def halves(ap, m, side):
            return ap.rearrange("p (b e m) -> p b e m", e=2, m=m)[:, :, side, :]

        def totals(g, m):
            if m == 1:
                t = g.F[:, :]
            else:
                at = S - 2 * (S // m)
                t = g.T[:, at:at + S // m]
            t = t.rearrange("p (b e) -> p b e", e=2)
            return t[:, :, 0:1], t[:, :, 1:2]

        def spread(t, m):
            return t.broadcast_to([P, S // (2 * m), m])

        def pe_product(pe, g, j, l):
            p = l % 2
            pe.wait_ge(g.lo_ready, 10 * j + l + 1)

            def part(out, s, t):
                return products(pe, out, g.kh[p][:, s], g.kl[p][:, s], g.qh[p][:, t], g.ql[p][:, t], True, True)

            if l < 8:
                if l >= 2:
                    pe.wait_ge(g.picked, 8 * j + l - 1)
                for b in range(SB):
                    mm = part(ps[:, p, b * P:(b + 1) * P], slice(b * P, (b + 1) * P), slice(b * P, (b + 1) * P))
            elif l == 8:
                part(ps[:, 2, 0:P], slice(0, P), slice(P, 2 * P))
                mm = part(ps[:, 2, P:2 * P], slice(2 * P, 3 * P), slice(3 * P, S))
            else:
                part(ps[:, 3, 0:2 * P], slice(0, P), slice(2 * P, S))
                mm = part(ps[:, 3, 2 * P:S], slice(P, 2 * P), slice(2 * P, S))
            mm.then_inc(g.prod_done, 1)

        def pe_hgrn_values(pe, g, j):
            pe.wait_ge(g.sdl_ready, j + 1)
            pe.wait_ge(g.fl_ready, j + 1)
            pe.wait_ge(g.v_ready, j + 1)
            off = {0: [(0, P, P), (2 * P, 2 * P, 2 * P)], 1: [(4 * P, 2 * P, 2 * P)], 2: [(P, 3 * P, P)], 3: []}
            for b in range(SB):
                s = slice(b * P, (b + 1) * P)
                mm = products(pe, ps[:, 4, s], g.vh[:, s], g.vl[:, s], g.sdh[:, b, :], g.sdl[:, b, :],
                              b == 0, b == SB - 1, skip_group_check=True)
                for at, t, n in off[b]:
                    products(pe, ps[:, 4, t:t + n], g.vh[:, s], g.vl[:, s], g.fh[:, at:at + n],
                             g.fl[:, at:at + n], False, False, skip_group_check=True)
            mm.then_inc(g.pv_done, 1)

        def pe_head(pe, g, i, attn, proj, x_ready=None):
            j = i - 1

            def turn_v():
                pe.wait_ge(g.vs_ready, i + 1)
                for b in range(SB):
                    mm = pe.transpose(ps[:, 2, b * P:(b + 1) * P], g.vs[:, b * P:(b + 1) * P], const("ident"))
                mm.then_inc(g.vT_done, 1)

            def at_step(c):
                if attn and c % 2 == 1 and c < 20:
                    pe_product(pe, g, j, c // 2)
                if attn and c == 25:
                    pe_hgrn_values(pe, g, j)
                if proj and c == 27:
                    turn_v()
                if attn and c == 29:
                    pe.wait_ge(g.sq_ready, j + 1)
                    pe.matmul(ps[:, 5, :], ones[:, :], g.sq[:, :], start=True, stop=True).then_inc(g.sum_done, 1)

            for k in range(4):
                if proj:
                    if k == 2:
                        pe.wait_ge(g.F_ready, i + 1)
                    if k == 3:
                        pe.wait_ge(g.Q_ready, i + 1)
                    if attn and k == 0:
                        pe.wait_ge(g.vs_ready, i)
                    if attn and k == 1:
                        pe.wait_ge(g.G_ready, i)
                    project(pe, g.ph, i, k, ps[:, 6 + k % 2, :], xh, xl, x_ready=x_ready if k == 0 else None,
                            between=lambda t, k=k: at_step(8 * k + t))
                else:
                    for t in range(KT):
                        at_step(8 * k + t)

        def act_level(act, g, j, l):
            p, m = l % 2, 1 << (l - 1) if l else 0
            if l == 0:
                act.wait_ge(g.start_ready, 2 * j + 2)
                q_src, k_src = g.Q[:, :], g.KG[:, :]
                q_dst, k_dst = g.qh[p][:, :], g.kh[p][:, :]
            else:
                if l >= 2:
                    act.wait_ge(g.uq_done, 8 * j + l - 1)
                    act.wait_ge(g.uk_done, 8 * j + l - 1)
                    act.wait_ge(g.prod_done, 10 * j + l - 1)
                q_src, k_src = halves(g.QF[:, :], m, 1), halves(g.KG[:, :], m, 0)
                q_dst, k_dst = halves(g.qh[p][:, :], m, 1), halves(g.kh[p][:, :], m, 0)
            act.activation(q_dst, q_src, ACT.Copy).then_inc(g.hi_ready, 1)
            act.activation(k_dst, k_src, ACT.Copy).then_inc(g.hi_ready, 1)

        def act_head(act, g, i, attn, proj):
            ph, j = g.ph, i - 1
            first = ph.first
            for l in range(10):
                if attn:
                    act_level(act, g, j, l)
                if proj and l == 4:
                    act.wait_ge(w_used, first + 4 * i + 1)
                    act.activation(g.sig[:, :], ps[:, 6, :], ACT.Sigmoid).then_inc(g.sigf_ready, 1)
                    split_hi(act, ph, i, 2)
                if proj and l == 8:
                    act.wait_ge(w_used, first + 4 * i + 2)
                    act.wait_ge(g.F_ready, i + 1)
                    act.activation(g.sig[:, :], ps[:, 7, :], ACT.Sigmoid).then_inc(g.sigq_ready, 1)
                    split_hi(act, ph, i, 3)
            if attn:
                act.wait_ge(g.picked, 8 * j + 8)
                act.activation(g.sdh[:, :, :], g.sd[:, :, :], ACT.Copy).then_inc(g.sdh_ready, 1)
                act.wait_ge(g.prod_done, 10 * j + 10)
                act.activation(g.fh[:, 0:2 * P], ps[:, 2, 0:2 * P], ACT.Copy).then_inc(g.fh_ready, 1)
                act.activation(g.fh[:, 2 * P:], ps[:, 3, :], ACT.Copy).then_inc(g.fh_ready, 1)
            if proj:
                act.wait_ge(w_used, first + 4 * i + 3)
                act.activation(g.vs[:, :], ps[:, 6, :], ACT.Copy).then_inc(g.vs_ready, 1)
                split_hi(act, ph, i, 4)
            if attn:
                act.wait_ge(g.pv_done, j + 1)
                act.activation(g.sq[:, :], ps[:, 4, :], ACT.Square).then_inc(g.sq_ready, 1)
            if proj:
                act.wait_ge(g.vT_done, i + 1)
                act.activation(g.vh[:, :], ps[:, 2, :], ACT.Copy).then_inc(g.vh_ready, 1)
            if attn:
                act.wait_ge(g.sum_done, j + 1)
                act.activation(g.root[:, :], ps[:, 5, :], ACT.Sqrt, scale=1.0 / P,
                               bias=small[:, 0:1]).then_inc(g.root_ready, 1)
            if proj:
                act.wait_ge(w_used, first + 4 * i + 4)
                act.wait_ge(g.Q_ready, i + 1)
                act.activation(g.sig[:, :], ps[:, 7, :], ACT.Sigmoid).then_inc(g.sigg_ready, 1)
                split_hi(act, ph, i, 5)

        def dve_level(dve, g, j, l):
            p, m = l % 2, 1 << (l - 1) if l else 0
            dve.wait_ge(g.hi_ready, 20 * j + 2 * l + 2)
            if l == 0:
                q_src, k_src = g.Q[:, :], g.KG[:, :]
                q_lo, k_lo, q_hi, k_hi = g.ql[p][:, :], g.kl[p][:, :], g.qh[p][:, :], g.kh[p][:, :]
            else:
                q_src, k_src = halves(g.QF[:, :], m, 1), halves(g.KG[:, :], m, 0)
                q_lo, k_lo = halves(g.ql[p][:, :], m, 1), halves(g.kl[p][:, :], m, 0)
                q_hi, k_hi = halves(g.qh[p][:, :], m, 1), halves(g.kh[p][:, :], m, 0)
            dve.tensor_tensor(q_lo, q_src, q_hi.bitcast(F32), ALU.subtract)
            dve.tensor_tensor(k_lo, k_src, k_hi.bitcast(F32), ALU.subtract).then_inc(g.lo_ready, 1)
            if 1 <= l <= 8:
                if l >= 2:
                    dve.wait_ge(g.ut_done, 7 * j + l - 1)
                left, _ = totals(g, m)
                q2 = halves(g.QF[:, :], m, 1)
                dve.tensor_tensor(q2, q2, spread(left, m), ALU.mult).then_inc(g.uq_done, 1)

        def dve_pick(dve, g, j, l):
            dve.wait_ge(g.prod_done, 10 * j + l + 1)
            if l:
                dve.wait_ge(g.picked, 8 * j + l)
            step(dve)
            mask = g.mask[:, l:l + 1, :].broadcast_to([P, SB, P])
            dve.copy_predicated(g.sd[:, :, :], mask, ps[:, l % 2, :].rearrange("p (b t) -> p b t", b=SB))\
               .then_inc(g.picked, 1)

        def dve_head(dve, g, i, attn, proj):
            ph, j = g.ph, i - 1
            first = ph.first
            if attn:
                dve.wait_ge(g.F_ready, i)
                dve.wait_ge(g.Q_ready, i)
                dve.tensor_scalar(g.KG[:, :], g.F[:, :], -1.0, 1.0, ALU.mult, ALU.add).then_inc(g.start_ready, 1)
                dve.tensor_tensor(g.QF[:, :], g.Q[:, :], g.F[:, :], ALU.mult).then_inc(g.start_ready, 1)
                dve.wait_ge(g.start_ready, 2 * i)
            for l in range(10):
                if attn:
                    dve_level(dve, g, j, l)
                    if 1 <= l <= 8:
                        dve_pick(dve, g, j, l - 1)
                if proj and l == 4:
                    at = bass.ds(i, 1) if not isinstance(i, int) else slice(i, i + 1)
                    dve.wait_ge(g.sigf_ready, i + 1)
                    if attn:
                        dve.wait_ge(g.ut_done, 7 * j + 1)
                        dve.wait_ge(g.uk_done, 8 * j + 1)
                    dve.tensor_scalar(g.F[:, :], g.sig[:, :], lbs[:, 1, at], lbs[:, 0, at], ALU.mult,
                                      ALU.add).then_inc(g.F_ready, 1)
                    split_lo(dve, ph, i, 2)
                if proj and l == 8:
                    dve.wait_ge(g.sigq_ready, i + 1)
                    dve.tensor_tensor(g.Q[:, :], g.sig[:, :], ps[:, 7, :], ALU.mult).then_inc(g.Q_ready, 1)
                    split_lo(dve, ph, i, 3)
            if attn:
                dve.wait_ge(g.fh_ready, 2 * j + 2)
                dve.tensor_tensor(g.fl[:, 0:2 * P], ps[:, 2, 0:2 * P], g.fh[:, 0:2 * P].bitcast(F32), ALU.subtract)
                dve.tensor_tensor(g.fl[:, 2 * P:], ps[:, 3, :], g.fh[:, 2 * P:].bitcast(F32),
                                  ALU.subtract).then_inc(g.fl_ready, 1)
                dve.wait_ge(g.sdh_ready, j + 1)
                dve.tensor_tensor(g.sdl[:, :, :], g.sd[:, :, :], g.sdh[:, :, :].bitcast(F32),
                                  ALU.subtract).then_inc(g.sdl_ready, 1)
            if proj:
                split_lo(dve, ph, i, 4)
                dve.wait_ge(g.vh_ready, i + 1)
                dve.tensor_tensor(g.vl[:, :], ps[:, 2, :], g.vh[:, :].bitcast(F32), ALU.subtract).then_inc(g.v_ready, 1)
            if attn:
                at = bass.ds(j, 1) if not isinstance(j, int) else slice(j, j + 1)
                dve.wait_ge(g.root_ready, j + 1)
                dve.reciprocal(g.rs[:, :], g.root[:, :]).then_inc(g.rs_ready, 1)
                dve.wait_ge(g.rs_ready, j + 1)
                dve.scalar_tensor_tensor(out=g.og[:, :], in0=ps[:, 4, :], scalar=vec[:, GN_AT:GN_AT + 1],
                                         in1=g.rs[:, :], op0=ALU.mult, op1=ALU.mult).then_inc(g.og_ready, 1)
                dve.wait_ge(g.og_ready, j + 1)
                dve.tensor_tensor(g.og[:, :], g.og[:, :], g.G[:, :], ALU.mult).then_inc(g.gated, 1)
                dve.wait_ge(g.gated, j + 1)
                oh = g.oh[:, at, :].rearrange("p a s -> p (a s)")
                ol = g.ol[:, at, :].rearrange("p a s -> p (a s)")
                dve.tensor_scalar(oh, g.og[:, :], 1.0, None, ALU.mult).then_inc(g.oh_ready, 1)
                dve.wait_ge(g.oh_ready, j + 1)
                dve.tensor_tensor(ol, g.og[:, :], oh.bitcast(F32), ALU.subtract).then_inc(g.o_ready, 1)
            if proj:
                dve.wait_ge(g.sigg_ready, i + 1)
                dve.tensor_tensor(g.G[:, :], g.sig[:, :], ps[:, 7, :], ALU.mult).then_inc(g.G_ready, 1)
                split_lo(dve, ph, i, 5)

        def pool_head(pool, g, j):
            for l in range(1, 9):
                m = 1 << (l - 1)
                left, right = totals(g, m)
                pool.wait_ge(g.lo_ready, 10 * j + l + 1)
                if l >= 2:
                    pool.wait_ge(g.ut_done, 7 * j + l - 1)
                k1 = halves(g.KG[:, :], m, 0)
                pool.tensor_tensor(k1, k1, spread(right, m), ALU.mult).then_inc(g.uk_done, 1)
                if l < 8:
                    at = S - 2 * (S // (2 * m))
                    out = g.T[:, at:at + S // (2 * m)].rearrange("p (b e) -> p b e", e=1)
                    pool.tensor_tensor(out, left, right, ALU.mult).then_inc(g.ut_done, 1)

        def hgrn_pe(pe, g, r):
            pe_head(pe, g, 0, False, True, x_ready=(r.x_ready, r.tiles))
            with pe.Fori(1, HG) as i:
                pe_head(pe, g, i, True, True)
            pe_head(pe, g, HG, True, False)

        def hgrn_act(act, g):
            act.wait_ge(g.lb_diff, 1)
            act.activation(lbs[:, 0, :], lbs[:, 1, :], ACT.Sigmoid).then_inc(g.lb_ready, 1)
            act_head(act, g, 0, False, True)
            with act.Fori(1, HG) as i:
                act_head(act, g, i, True, True)
            act_head(act, g, HG, True, False)

        def hgrn_dve(dve, g):
            lb0, lb1 = (vec[:, VEC_AT[n]:VEC_AT[n] + KT] for n in ("lb0", "lb1"))
            dve.tensor_tensor(lbs[:, 1, :], lb0, lb1, ALU.subtract).then_inc(g.lb_diff, 1)
            dve.wait_ge(g.lb_ready, 1)
            dve.tensor_scalar(lbs[:, 1, :], lbs[:, 0, :], -1.0, 1.0, ALU.mult, ALU.add).then_inc(g.lb_ready, 1)
            dve.wait_ge(g.lb_ready, 2)
            dve.wait_ge(g.masks_in, 16)
            dve.wait_ge(g.cleared, 5)
            dve_head(dve, g, 0, False, True)
            with dve.Fori(1, HG) as i:
                dve_head(dve, g, i, True, True)
            dve_head(dve, g, HG, True, False)

        def hgrn_pool(pool, g):
            pool.memset(g.sd[:, :, :], 0.0).then_inc(g.cleared, 1)
            for t in (g.qh[1], g.ql[1], g.kh[1], g.kl[1]):
                pool.memset(t[:, :].bitcast(F32), 0.0).then_inc(g.cleared, 1)
            pool.dma_start(g.mask[:, :, :], levels).then_inc(g.masks_in, 16)
            with pool.Fori(0, HG) as j:
                pool_head(pool, g, j)

        small_ops = sem("small_ops")
        stick = Pairs("stick", PH["stick"])
        up0 = Up("up0", PH["up0"])
        dil = Pairs("dilated", PH["dilated"])
        up1 = Up("up1", PH["up1"])
        hg = Hgrn(PH["hgrn"])
        up2 = Up("up2", PH["up2"], 0)
        win = Pairs("window", PH["window"])
        up3 = Up("up3", PH["up3"], 1)
        o_stick = Out(PH["stick_out"], stick.oh, stick.ol)
        o_up0 = Out(PH["down0"], up0.ah, up0.al)
        o_dil = Out(PH["dilated_out"], dil.oh, dil.ol)
        o_up1 = Out(PH["down1"], up1.ah, up1.al)
        o_hg = Out(PH["hgrn_out"], hg.oh, hg.ol)
        o_up2 = Out(PH["down2"], up2.ah, up2.al)
        o_win = Out(PH["window_out"], win.oh, win.ol)
        o_up3 = Out(PH["down3"], up3.ah, up3.al)
        r_in = Rms(0, "mix0", None)
        r_ffn0 = Rms(1, "ffn0", o_stick)
        r_mix1 = Rms(2, "mix1", o_up0)
        r_ffn1 = Rms(3, "ffn1", o_dil)
        r_fin = Rms(4, "final", o_up1)
        fin_scaled = sem("fin_scaled")
        l_mix0 = Layer(0, "lnmg0", "lnmb0")
        l_ffn0 = Layer(1, "lnfg0", "lnfb0")
        l_mix1 = Layer(2, "lnmg1", "lnmb1")
        l_ffn1 = Layer(3, "lnfg1", "lnfb1")
        table, one_hot, rows = stick.table, stick.one_hot, stick.rows
        up_sq, up_mu = up0.sq, up0.mu
        bias_rows_ready, bias_written, bias_loaded = sem("bias_rows"), sem("bias_written"), sem("bias_loaded")
        sinks_in, sinks_neg = sem("sinks_in"), sem("sinks_neg")

        @block.sync
        def _(sp):
            for k in range(2):
                fetch(sp, PH["stick"], 0, k, wait=False)
            for j in range(KT):
                sp.dma_start(hT[:, j, :], x_t[j * P:(j + 1) * P, :]).then_inc(x_in, 16)
            for dst, src in ((vec[:, :], vectors), (cst[:, :], consts), 
                             (cvt[:, :, :, :], conv), (stick.resets[:, :], resets)):
                sp.dma_start(dst, src).then_inc(loaded, 16)
            fetch(sp, PH["stick"], 0, 2)
            with sp.Fori(1, PAIRS) as i:
                for k in range(3):
                    fetch(sp, PH["stick"], i, k)
            for o, up in ((o_stick, "up0"), (o_up0, "dilated"), (o_dil, "up1"), (o_up1, "hgrn"),
                          (o_hg, "up2"), (o_up2, "window"), (o_win, "up3"), (o_up3, None)):
                o.fetches(sp)
                if up is not None:
                    ph = PH[up]
                    with sp.Fori(0, ph.iters) as i:
                        for k in range(len(ph.slots)):
                            fetch(sp, ph, i, k)
            for j in range(KT):
                sp.wait_ge(l_ffn1.h_new, l_ffn1.tiles + j + 1)
                sp.dma_start(out_t[j * P:(j + 1) * P, :], hT[:, j, :]).then_inc(out_done, 16)
            sp.wait_ge(out_done, 16 * KT)

        @block.gpsimd
        def _(pool):
            pool.memset(ones[:, :], 1.0).then_inc(ones_made, 1)
            pool.memset(small[:, 0:1], RMS_EPS).then_inc(ones_made, 1)
            pool.memset(tiny[:, :], 0.0).then_inc(ones_made, 1)
            pool.memset(small[:, 1:2], LN_EPS).then_inc(ones_made, 1)
            pool.memset(stick.left[:, TRI:TRI + 1], 0.0).then_inc(ones_made, 1)
            for v in (stick.vh, stick.vl):
                pool.memset(v[:, :, :, :].bitcast(F32), 0.0).then_inc(stick.padded.sem, 1)
            pool.dma_start(table[0:BUCKETS, :], buckets).then_inc(sinks_in, 16)
            pool.dma_start(one_hot[0:BUCKETS + 1, :], onehot).then_inc(sinks_in, 16)
            pool.wait_ge(*stick.padded(2))
            pool.memset(table[BUCKETS:BUCKETS + 1, :], NEG).then_inc(sinks_neg, 1)
            pool.wait_ge(*o_up0.tile_done(KT))
            for v in (dil.vh, dil.vl):
                pool.memset(v[:, :, :, :].bitcast(F32), 0.0).then_inc(dil.padded.sem, 1)
            pool.wait_ge(loaded, 16 * 4)
            pool_pair(pool, dil, 0)
            with pool.Fori(1, PAIRS) as i:
                pool_pair(pool, dil, i)
            pool.wait_ge(*o_up1.tile_done(KT))
            hgrn_pool(pool, hg)
            pool.wait_ge(*o_up2.tile_done(KT))
            for v in (win.vh, win.vl):
                pool.memset(v[:, :, :, :].bitcast(F32), 0.0).then_inc(win.padded.sem, 1)
            pool.wait_ge(bias_written, 16)
            windows = bass.AP(tensor=scratch.tensor, offset=0,
                              ap=[[1, P], [3 * WINDOW, HEADS], [1, 2 * WINDOW]])
            pool.dma_start(win.bias[:, :, :], windows).then_inc(bias_loaded, 16)
            pool.dma_start(win.sink[:, :], sinks).then_inc(bias_loaded, 16)

        def attention_pe(pe, a, r, stats_bank):
            pe_pair(pe, a, 0, False, True, x_ready=(r.x_ready, r.tiles),
                    stats=None if stats_bank is None else lambda: rms_pe(pe, r, stats_bank))
            pe.wait_ge(*a.padded(2))
            with pe.Fori(1, PAIRS) as i:
                pe_pair(pe, a, i, True, True)
            pe_pair(pe, a, PAIRS, True, False)

        @block.tensor
        def _(pe):
            pe.wait_ge(ones_made, 5)
            pe.wait_ge(loaded, 16 * 4)
            pe.wait_ge(sinks_in, 32)
            pe.wait_ge(sinks_neg, 1)
            pe.matmul(ps[0:HEADS, 4, 0:3 * WINDOW], table[0:BUCKETS + 1, :], one_hot[0:BUCKETS + 1, :],
                      start=True, stop=True).then_inc(small_ops, 1)
            attention_pe(pe, stick, r_in, 5)
            o_stick.pe(pe, lambda e: e.wait_ge(*stick.o_ready(PAIRS)))
            up_pe(pe, up0, r_ffn0, lambda: rms_pe(pe, r_ffn0, 5))
            o_up0.pe(pe, lambda e: e.wait_ge(*up0.a_ready(FT)))
            attention_pe(pe, dil, r_mix1, 5)
            o_dil.pe(pe, lambda e: e.wait_ge(*dil.o_ready(PAIRS)))
            up_pe(pe, up1, r_ffn1, lambda: rms_pe(pe, r_ffn1, 5))
            o_up1.pe(pe, lambda e: e.wait_ge(*up1.a_ready(FT)))
            rms_pe(pe, r_fin, 0)
            hgrn_pe(pe, hg, r_fin)
            o_hg.pe(pe, lambda e: e.wait_ge(hg.o_ready, HG))
            layer_pe(pe, l_mix0)
            up_pe(pe, up2, l_mix0, None)
            o_up2.pe(pe, lambda e: e.wait_ge(*up2.a_ready(FT)))
            layer_pe(pe, l_ffn0)
            attention_pe(pe, win, l_ffn0, None)
            o_win.pe(pe, lambda e: e.wait_ge(*win.o_ready(PAIRS)))
            layer_pe(pe, l_mix1)
            up_pe(pe, up3, l_mix1, None)
            o_up3.pe(pe, lambda e: e.wait_ge(*up3.a_ready(FT)))
            layer_pe(pe, l_ffn1)

        def attention_act(act, a, r, last_wait=None):
            act_pair(act, a, 0, False, True)
            with act.Fori(1, PAIRS) as i:
                act_pair(act, a, i, True, True)
            act_pair(act, a, PAIRS, True, False)

        @block.scalar
        def _(act):
            act.wait_ge(loaded, 16 * 4)
            act.wait_ge(ones_made, 5)
            act.activation(identr[:, :], const("ident"), ACT.Copy).then_inc(consts_made, 1)
            act.activation(maskr[:, :], const("diagmask"), ACT.Copy).then_inc(consts_made, 1)
            for k in range(2):
                split_hi(act, PH["stick"], 0, k, wait=False)
            rms_act_x(act, r_in, range(KT))
            act.wait_ge(small_ops, 1)
            act.activation(rows[0:HEADS, :], ps[0:HEADS, 4, 0:3 * WINDOW], ACT.Copy).then_inc(bias_rows_ready, 1)
            act.wait_ge(bias_rows_ready, 1)
            act.dma_start(scratch, rows[0:HEADS, :]).then_inc(bias_written, 16)
            rms_act_sq(act, r_in, stick.sq, range(KT))
            rms_act_root(act, r_in, 5, D, 0)
            attention_act(act, stick, r_in)
            act.wait_ge(bias_written, 16)
            Out_then_rms(o_stick, r_ffn0, up_sq).act(act)
            rms_act_root(act, r_ffn0, 5, D, 0)
            up_act(act, up0)
            Out_then_rms(o_up0, r_mix1, up_sq).act(act)
            for j in range(KT):
                if j == 0:
                    act.wait_ge(*o_up0.tile_done(KT))
                act.activation(dil.x2h[:, j, :], hT[:, j, :], ACT.Copy, scale=gain("kv", j)).then_inc(dil.x2h_done, 1)
            rms_act_root(act, r_mix1, 5, D, 0)
            attention_act(act, dil, r_mix1)
            Out_then_rms(o_dil, r_ffn1, up_sq).act(act)
            rms_act_root(act, r_ffn1, 5, D, 0)
            up_act(act, up1)
            for half in range(2):
                o_up1.splits(split_hi, act, half)
                for j in range(half * 4, half * 4 + 4):
                    h_wait(act, o_up1, j)
                    if j >= 2:
                        act.wait_ge(r_fin.acc_done, r_fin.tiles + j - 1)
                    act.activation(up_sq[:, j % 2, :], hT[:, j, :], ACT.Square).then_inc(r_fin.sq_done, 1)
            rms_act_root(act, r_fin, 0, D, 0)
            for j in range(KT):
                act.wait_ge(fin_scaled, j + 1)
                act.activation(xh[:, j, :], hT[:, j, :], ACT.Copy).then_inc(r_fin.xh_done, 1)
            hgrn_act(act, hg)
            layer_act(act, o_hg, l_mix0, up_mu, up_sq)
            up_act(act, up2)
            layer_act(act, o_up2, l_ffn0, up_mu, up_sq)
            attention_act(act, win, l_ffn0)
            layer_act(act, o_win, l_mix1, up_mu, up_sq)
            up_act(act, up3)
            layer_act(act, o_up3, l_ffn1, up_mu, up_sq)

        def attention_dve(dve, a):
            dve_pair(dve, a, 0, False, True)
            with dve.Fori(1, PAIRS) as i:
                dve_pair(dve, a, i, True, True)
            dve_pair(dve, a, PAIRS, True, False)

        @block.vector
        def _(dve):
            dve.wait_ge(loaded, 16 * 4)
            dve.wait_ge(ones_made, 5)
            dve.wait_ge(consts_made, 2)
            for k in range(2):
                split_lo(dve, PH["stick"], 0, k)
            for j in range(KT):
                h_wait(dve, None, j)
                rms_dve_x(dve, r_in, j)
            rms_dve_acc(dve, r_in, stick.sq, range(KT))
            rms_dve_rstd(dve, r_in)
            dve.wait_ge(r_in.rstd_ready, r_in.n + 1)
            attention_dve(dve, stick)
            Out_then_rms(o_stick, r_ffn0, up_sq).dve(dve)
            rms_dve_rstd(dve, r_ffn0)
            dve.wait_ge(r_ffn0.rstd_ready, r_ffn0.n + 1)
            up_dve(dve, up0)
            Out_then_rms(o_up0, r_mix1, up_sq).dve(dve)
            for j in range(KT):
                dve.wait_ge(dil.x2h_done, j + 1)
                dve.scalar_tensor_tensor(out=dil.x2l[:, j, :], in0=hT[:, j, :], scalar=gain("kv", j),
                                         in1=dil.x2h[:, j, :].bitcast(F32), op0=ALU.mult,
                                         op1=ALU.subtract).then_inc(dil.x2_ready, 1)
            rms_dve_rstd(dve, r_mix1)
            dve.wait_ge(r_mix1.rstd_ready, r_mix1.n + 1)
            attention_dve(dve, dil)
            Out_then_rms(o_dil, r_ffn1, up_sq).dve(dve)
            rms_dve_rstd(dve, r_ffn1)
            dve.wait_ge(r_ffn1.rstd_ready, r_ffn1.n + 1)
            up_dve(dve, up1)
            for half in range(2):
                o_up1.splits(split_lo, dve, half)
                add_half(dve, o_up1, half)
                rms_dve_acc(dve, r_fin, up_sq, range(half * 4, half * 4 + 4))
            rms_dve_rstd(dve, r_fin)
            dve.wait_ge(r_fin.rstd_ready, r_fin.n + 1)

            def low(j):
                dve.wait_ge(r_fin.xh_done, r_fin.tiles + j + 1)
                dve.tensor_tensor(xl[:, j, :], hT[:, j, :], xh[:, j, :].bitcast(F32),
                                  ALU.subtract).then_inc(r_fin.x_ready, 1)

            for j in range(KT):
                dve.scalar_tensor_tensor(out=hT[:, j, :], in0=hT[:, j, :], scalar=gain("final", j),
                                         in1=rstd[:, :], op0=ALU.mult, op1=ALU.mult).then_inc(fin_scaled, 1)
                if j:
                    low(j - 1)
            low(KT - 1)
            hgrn_dve(dve, hg)
            layer_dve(dve, o_hg, l_mix0, up_mu, up_sq)
            up_dve(dve, up2)
            layer_dve(dve, o_up2, l_ffn0, up_mu, up_sq)
            dve.wait_ge(bias_loaded, 32)
            dve.wait_ge(*win.padded(2))
            dve.tensor_scalar(win.negsink[:, :], win.sink[:, :], -1.0, None, ALU.mult).then_inc(sinks_neg, 1)
            dve.wait_ge(sinks_neg, 2)
            attention_dve(dve, win)
            layer_dve(dve, o_win, l_mix1, up_mu, up_sq)
            up_dve(dve, up3)
            layer_dve(dve, o_up3, l_ffn1, up_mu, up_sq)


def constants():
    q = np.arange(P)
    table = np.zeros((P, CONST_COLS), np.float32)

    def put(name, a):
        at, w = CONST_AT[name]
        table[:, at:at + w] = a

    put("ident", np.eye(P, dtype=np.float32))
    put("diagmask", np.where(q[None, :] >= q[:, None], np.float32(NEG), np.float32(0.0)))
    rot = np.zeros((P, P), np.float32)
    for d in range(P):
        if d % HD < HD // 2:
            rot[d + HD // 2, d] = -1.0
        else:
            rot[d - HD // 2, d] = 1.0
    put("rot", rot)
    dist = (S - P + q)[:, None] - np.arange(S)[None, :]
    n = ((dist >= 0) & (dist <= 128)).astype(int) + ((dist >= 0) & (dist % 4 == 0)) + ((dist >= 0) & (dist % 16 == 0))
    put("count", np.where(n > 0, np.log(np.maximum(n, 1)), NEG).astype(np.float32))
    freq = np.float32(10000.0) ** (-np.arange(0, HD, 2, dtype=np.float32) / np.float32(HD))
    angle = (np.arange(S, dtype=np.float32)[None, :] * freq[:, None]).astype(np.float32)
    row = np.arange(P) % (HD // 2)
    put("cos", np.cos(angle.astype(np.float64)).astype(np.float32)[row])
    put("sin", np.sin(angle.astype(np.float64)).astype(np.float32)[row])
    levels = np.zeros((P, LEVELS, P), np.int32)
    levels[:, 0, :] = np.eye(P)
    for l in range(1, LEVELS):
        m = 1 << (l - 1)
        left = (q // m) % 2 == 0
        levels[:, l, :] = left[:, None] & (q[None, :] // m == (q // m)[:, None] + 1)
    resets = np.zeros((P, TRI), np.float32)
    for i in range(SB):
        resets[:, Q_AT[i] + (i + 1) * P - 1] = 1.0
    hot = np.zeros((BUCKETS + 1, 3 * WINDOW), np.float32)
    exact = BUCKETS // 2
    for y in range(3 * WINDOW):
        d = 2 * WINDOW - 1 - y
        if 0 <= d < WINDOW:
            far = exact + int(np.log(np.float32(max(d, 1)) / exact) / np.log(MAX_DIST / exact) * (BUCKETS - exact))
            hot[d if d < exact else min(far, BUCKETS - 1), y] = 1.0
        else:
            hot[BUCKETS, y] = 1.0
    return table, levels, resets, hot


def kernel(x, norm_mix, w_qkv_a, w_o_a, norm_kv, w_kv, w_q_b, w_o_b, norm_ffn, w_gate, w_up, w_down, norm_final,
           hgrn_w_in_2, hgrn_lb_logits_2, hgrn_gnorm_w_2, hgrn_w_out_2, swa_w_q_2, swa_sinks_2, swa_w_out_2,
           shared_w_kv_2, rel_bias_2, ffn_w_in_2, ffn_conv_w_2, ffn_conv_b_2, ffn_w_out_2, ln_mix_g_2,
           ln_mix_b_2, ln_ffn_g_2, ln_ffn_b_2):
    from concourse import bacc
    from concourse.bass_utils import run_bass_kernel_spmd

    def host(a):
        return np.ascontiguousarray(a)

    def columns(w):
        w = host(w)
        return w.reshape(KT, P, w.shape[1] // P, P).transpose(2, 1, 0, 3).reshape(-1, P, SLAB)

    def halves(w):
        w = host(w)
        return w.reshape(w.shape[0] // (2 * P), 2, P, 2, S).transpose(3, 0, 2, 1, 4).reshape(-1, P, SLAB)

    def interleave(*parts):
        return np.stack(parts, axis=1).reshape(-1, P, SLAB)

    def twice(w):
        w = host(w).reshape(D, 4, 1, HD)
        return columns(np.broadcast_to(w, (D, 4, 4, HD)).reshape(D, D))

    qkv, kv = host(w_qkv_a)[0], host(w_kv)
    hin = host(hgrn_w_in_2)[0]
    skv = host(shared_w_kv_2)
    fin = host(ffn_w_in_2)
    stream = [
        interleave(columns(qkv[:, :D]), columns(qkv[:, D:2 * D]), columns(qkv[:, 2 * D:])), halves(host(w_o_a)[0]),
        interleave(columns(host(w_gate)[0]), columns(host(w_up)[0])), halves(host(w_down)[0]),
        interleave(columns(host(w_q_b)[0]), columns(kv[:, :D]), columns(kv[:, D:])), halves(host(w_o_b)[0]),
        interleave(columns(host(w_gate)[1]), columns(host(w_up)[1])), halves(host(w_down)[1]),
        interleave(columns(hin[:, D:2 * D]), columns(hin[:, :D]), columns(hin[:, 2 * D:3 * D]), columns(hin[:, 3 * D:])),
        halves(host(hgrn_w_out_2)[0]),
        interleave(columns(fin[0][:, :FF]), columns(fin[0][:, FF:])), halves(host(ffn_w_out_2)[0]),
        interleave(columns(host(swa_w_q_2)[0]), twice(skv[:, :4 * HD]), twice(skv[:, 4 * HD:])),
        halves(host(swa_w_out_2)[0]),
        interleave(columns(fin[1][:, :FF]), columns(fin[1][:, FF:])), halves(host(ffn_w_out_2)[1]),
    ]
    weights = host(np.concatenate(stream, axis=0))
    assert weights.shape[0] == TOTAL_SLABS

    def vector(v):
        return host(v).reshape(KT, P).T

    lb = host(hgrn_lb_logits_2)
    mix, ffn = host(norm_mix), host(norm_ffn)
    lists = [mix[0], mix[1], host(norm_kv), ffn[0], ffn[1], host(norm_final), lb[0], lb[1]]
    for g, b in ((host(ln_mix_g_2), host(ln_mix_b_2)), (host(ln_ffn_g_2), host(ln_ffn_b_2))):
        lists += [g[0], b[0], g[1], b[1]]
    vectors = host(np.concatenate([vector(v) for v in lists] + [host(hgrn_gnorm_w_2)[0].reshape(P, 1)], axis=1))
    taps = np.concatenate([host(ffn_conv_w_2), host(ffn_conv_b_2)[:, None, :]], axis=1)
    conv = host(taps.reshape(2, 4, 2 * FT, P).transpose(3, 0, 2, 1))
    consts, levels, resets, hot = constants()
    arrays = {
        "x_t": host(host(x)[0].T), "weights": weights, "vectors": vectors, "conv": conv, "consts": consts,
        "levels": levels, "resets": resets,
        "sinks": host(np.broadcast_to(host(swa_sinks_2)[0][None, :], (P, HEADS))),
        "buckets": host(rel_bias_2), "onehot": hot,
    }
    nc = bacc.Bacc("TRN2", target_bir_lowering=False, num_devices=1)
    aps = {n: nc.dram_tensor(n, a.shape, mybir.dt.from_np(a.dtype), kind="ExternalInput").ap()
           for n, a in arrays.items()}
    out_t = nc.dram_tensor("out_t", (D, S), F32, kind="ExternalOutput").ap()
    program(nc, out_t=out_t, **aps)
    r = run_bass_kernel_spmd(nc, [arrays], core_ids=[0])
    return host(r.results[0]["out_t"].T).reshape(1, S, D)
```
